# Optimizing a Trainium2 kernel written in Bass

```python
import jax, jax.numpy as jnp
from jax import lax
import numpy as np
import jax
import jax.numpy as jnp

D_MODEL = 1024
BATCH = 1
SEQ = 512
DEPTH = 1

N_MEM = 256
HEAD_DIM = 64
ATTN_WIDTH = D_MODEL // 2
CONV_WIDTH = D_MODEL // 4
XATTN_WIDTH = D_MODEL // 4
N_ATTN_HEADS = ATTN_WIDTH // HEAD_DIM
N_XATTN_HEADS = 4
XATTN_HEAD_DIM = XATTN_WIDTH // N_XATTN_HEADS
MIX_WIDTH = ATTN_WIDTH + CONV_WIDTH + XATTN_WIDTH
IN_PROJ_WIDTH = 3 * ATTN_WIDTH + 3 * CONV_WIDTH + XATTN_WIDTH
DILATED_PATTERNS = ((128, 1), (512, 4), (2048, 16))
CONV_K = 3
D_FF = 4 * D_MODEL
ROPE_THETA = 10000.0
EPS = 1e-6
NEG_INF = -1e30


def rms_norm(x, g):
    xf = x.astype(jnp.float32)
    y = xf * lax.rsqrt(jnp.mean(xf * xf, axis=-1, keepdims=True) + EPS)
    return (y * g.astype(jnp.float32)).astype(x.dtype)

def apply_rope(t, positions):
    dh = t.shape[-1]
    half = dh // 2
    inv_freq = jnp.float32(ROPE_THETA) ** (-(jnp.arange(half, dtype=jnp.float32) * 2.0 / dh))
    ang = positions.astype(jnp.float32)[..., None] * inv_freq
    cos = jnp.cos(ang)[:, :, None, :]
    sin = jnp.sin(ang)[:, :, None, :]
    tf = t.astype(jnp.float32)
    t1, t2 = tf[..., :half], tf[..., half:]
    out = jnp.concatenate([t1 * cos - t2 * sin, t1 * sin + t2 * cos], axis=-1)
    return out.astype(t.dtype)

def dilated_window_attention(q, k, v, window, dilation):
    B, S, H, Dh = q.shape
    L = S // dilation
    n_back = window // dilation
    blk = n_back
    nb = -(-L // blk)
    Lp = nb * blk

    def to_blocks(t):
        t = t.reshape(B, L, dilation, H, Dh).transpose(0, 2, 1, 3, 4)
        t = jnp.pad(t, ((0, 0), (0, 0), (0, Lp - L), (0, 0), (0, 0)))
        return t.reshape(B, dilation, nb, blk, H, Dh)

    qb, kb, vb = to_blocks(q), to_blocks(k), to_blocks(v)

    def with_prev(t):
        prev = jnp.pad(t, ((0, 0), (0, 0), (1, 0), (0, 0), (0, 0), (0, 0)))[:, :, :-1]
        return jnp.concatenate([prev, t], axis=3)

    kw, vw = with_prev(kb), with_prev(vb)
    scale = Dh ** -0.5
    s = jnp.einsum('bdnqhc,bdnkhc->bdnhqk', qb, kw,
                   preferred_element_type=jnp.float32) * scale
    qi = jnp.arange(blk)[:, None]
    kj = jnp.arange(2 * blk)[None, :]
    band = (kj >= qi) & (kj <= qi + n_back)
    valid = band[None] & ((jnp.arange(nb)[:, None, None] > 0) | (kj[None] >= blk))
    s = jnp.where(valid[None, None, :, None], s, NEG_INF)
    lse = jax.nn.logsumexp(s, axis=-1)
    p = jnp.exp(s - lse[..., None])
    o = jnp.einsum('bdnhqk,bdnkhc->bdnqhc', p.astype(v.dtype), vw,
                   preferred_element_type=jnp.float32)
    o = o.reshape(B, dilation, Lp, H, Dh)[:, :, :L]
    o = o.transpose(0, 2, 1, 3, 4).reshape(B, S, H, Dh)
    lse = lse.transpose(0, 1, 2, 4, 3).reshape(B, dilation, Lp, H)[:, :, :L]
    lse = lse.transpose(0, 2, 1, 3).reshape(B, S, H)
    return o, lse

def dilated_mixture_attention(q, k, v):
    outs, lses = [], []
    for window, dilation in DILATED_PATTERNS:
        o, lse = dilated_window_attention(q, k, v, window, dilation)
        outs.append(o)
        lses.append(lse)
    w = jax.nn.softmax(jnp.stack(lses, axis=0), axis=0)
    o = jnp.sum(w[..., None] * jnp.stack(outs, axis=0), axis=0)
    return o.astype(q.dtype)

def short_gated_conv(b_gate, c_gate, u, conv_w):
    z = c_gate * u
    S = z.shape[1]
    zp = jnp.pad(z, ((0, 0), (CONV_K - 1, 0), (0, 0)))
    y = zp[:, 0:S] * conv_w[0]
    for tap in range(1, CONV_K):
        y = y + zp[:, tap:tap + S] * conv_w[tap]
    return b_gate * y

def memory_cross_attention(qx, mem_kv):
    B, S, _ = qx.shape
    q = qx.reshape(B, S, N_XATTN_HEADS, XATTN_HEAD_DIM)
    km, vm = jnp.split(mem_kv, 2, axis=-1)
    km = km.reshape(B, -1, N_XATTN_HEADS, XATTN_HEAD_DIM)
    vm = vm.reshape(B, -1, N_XATTN_HEADS, XATTN_HEAD_DIM)
    s = jnp.einsum('bshc,bmhc->bhsm', q, km,
                   preferred_element_type=jnp.float32) * (XATTN_HEAD_DIM ** -0.5)
    p = jax.nn.softmax(s, axis=-1)
    o = jnp.einsum('bhsm,bmhc->bshc', p.astype(vm.dtype), vm)
    return o.reshape(B, S, XATTN_WIDTH)

def first_inputs(seed: int = 0) -> dict:
    key = jax.random.key(seed)
    ks = jax.random.split(key, 20)
    f32 = jnp.float32

    def w(k, shape, fan_in):
        return jax.random.normal(k, shape, f32) * (fan_in ** -0.5)

    def gain(k, width):
        return 1.0 + 0.05 * jax.random.normal(k, (DEPTH, width), f32)

    x = jax.random.normal(ks[0], (BATCH, SEQ, D_MODEL), f32)
    mem = jax.random.normal(ks[1], (BATCH, N_MEM, D_MODEL), f32)
    offset = jax.random.randint(ks[2], (BATCH, 1), 0, 1024, dtype=jnp.int32)
    positions = offset + jnp.arange(SEQ, dtype=jnp.int32)[None, :]
    return {
        "x": x,
        "mem": mem,
        "positions": positions,
        "g_pre_mix": gain(ks[3], D_MODEL),
        "g_mem": gain(ks[4], D_MODEL),
        "w_in": w(ks[5], (DEPTH, D_MODEL, IN_PROJ_WIDTH), D_MODEL),
        "w_mem_kv": w(ks[6], (DEPTH, D_MODEL, 2 * XATTN_WIDTH), D_MODEL),
        "conv_w": w(ks[7], (DEPTH, CONV_K, CONV_WIDTH), CONV_K),
        "g_attn_out": gain(ks[8], ATTN_WIDTH),
        "g_conv_out": gain(ks[9], CONV_WIDTH),
        "g_xattn_out": gain(ks[10], XATTN_WIDTH),
        "w_out": w(ks[11], (DEPTH, MIX_WIDTH, D_MODEL), MIX_WIDTH),
        "g_post_mix": gain(ks[12], D_MODEL),
        "g_pre_mlp": gain(ks[13], D_MODEL),
        "w_up": w(ks[14], (DEPTH, D_MODEL, D_FF), D_MODEL),
        "w_down": w(ks[15], (DEPTH, D_FF, D_MODEL), D_FF),
        "g_post_mlp": gain(ks[16], D_MODEL),
    }

def first_block(x, mem, positions, g_pre_mix, g_mem, w_in, w_mem_kv, conv_w,
              g_attn_out, g_conv_out, g_xattn_out, w_out, g_post_mix,
              g_pre_mlp, w_up, w_down, g_post_mlp):
    B, S, _ = x.shape
    a0 = ATTN_WIDTH
    c0 = 3 * ATTN_WIDTH
    x0 = 3 * ATTN_WIDTH + 3 * CONV_WIDTH
    for l in range(DEPTH):
        h = rms_norm(x, g_pre_mix[l])
        proj = jnp.einsum('bsd,de->bse', h, w_in[l])

        q = proj[..., 0:a0].reshape(B, S, N_ATTN_HEADS, HEAD_DIM)
        k = proj[..., a0:2 * a0].reshape(B, S, N_ATTN_HEADS, HEAD_DIM)
        v = proj[..., 2 * a0:3 * a0].reshape(B, S, N_ATTN_HEADS, HEAD_DIM)
        q = apply_rope(q, positions)
        k = apply_rope(k, positions)
        y_attn = dilated_mixture_attention(q, k, v).reshape(B, S, ATTN_WIDTH)

        b_gate = proj[..., c0:c0 + CONV_WIDTH]
        c_gate = proj[..., c0 + CONV_WIDTH:c0 + 2 * CONV_WIDTH]
        u = proj[..., c0 + 2 * CONV_WIDTH:c0 + 3 * CONV_WIDTH]
        y_conv = short_gated_conv(b_gate, c_gate, u, conv_w[l])

        qx = proj[..., x0:x0 + XATTN_WIDTH]
        mem_kv = jnp.einsum('bmd,de->bme', rms_norm(mem, g_mem[l]), w_mem_kv[l])
        y_x = memory_cross_attention(qx, mem_kv)

        y = jnp.concatenate([rms_norm(y_attn, g_attn_out[l]),
                             rms_norm(y_conv, g_conv_out[l]),
                             rms_norm(y_x, g_xattn_out[l])], axis=-1)
        y = jnp.einsum('bse,ed->bsd', y, w_out[l])
        x = x + rms_norm(y, g_post_mix[l])

        h2 = rms_norm(x, g_pre_mlp[l])
        f = jnp.square(jax.nn.relu(jnp.einsum('bsd,df->bsf', h2, w_up[l])))
        f = jnp.einsum('bsf,fd->bsd', f, w_down[l])
        x = x + rms_norm(f, g_post_mlp[l])
    return x


GRID_W = 64
CTX_LEN = 256
N_MOD = 6

MLA_V = 128
MLA_HEADS = D_MODEL // MLA_V
MLA_NOPE = 128
MLA_ROPE = 64
MLA_QK = MLA_NOPE + MLA_ROPE
MLA_Q_RANK = 3 * D_MODEL // 4
MLA_KV_RANK = D_MODEL // 4
MLA_WIDTH = MLA_HEADS * MLA_V
ROPE_BASE = 10000.0
Q_BLOCK = 128

HG_DK = 128
HG_HEADS = D_MODEL // HG_DK
HG_DV = D_MODEL // HG_HEADS
HG_FDIM = HG_HEADS * HG_DK
HG_WIDTH = HG_HEADS * HG_DV
HG_CHUNK = 64

N_EXPERTS = 32
TOP_K = 4
D_EXPERT = D_MODEL
SWIGLU_LIMIT = 7.0
SWIGLU_ALPHA = 1.702
MOE_BLOCK = 128

IN_SPLITS = (MLA_Q_RANK, MLA_KV_RANK + MLA_ROPE, HG_FDIM, HG_FDIM, HG_FDIM, HG_WIDTH, HG_WIDTH, D_MODEL, D_MODEL)
D_IN = MLA_Q_RANK + MLA_KV_RANK + MLA_ROPE + 3 * HG_FDIM + 2 * HG_WIDTH + 2 * D_MODEL


def rmsnorm(x, g):
    xf = x.astype(jnp.float32)
    y = xf * lax.rsqrt(jnp.mean(xf * xf, axis=-1, keepdims=True) + EPS)
    return (y * g.astype(jnp.float32)).astype(x.dtype)

def split_cols(p):
    return jnp.split(p, np.cumsum(IN_SPLITS)[:-1].tolist(), axis=-1)

def axial_rope_tables(rows):
    row = jnp.repeat(jnp.arange(rows), GRID_W).astype(jnp.float32)
    col = jnp.tile(jnp.arange(GRID_W), rows).astype(jnp.float32)
    n_freq = MLA_ROPE // 4
    inv = ROPE_BASE ** (-jnp.arange(n_freq, dtype=jnp.float32) / n_freq)
    ang = jnp.concatenate([row[:, None] * inv, col[:, None] * inv], axis=-1)
    return jnp.cos(ang), jnp.sin(ang)

def apply_rope_2(x, cos, sin):
    half = MLA_ROPE // 2
    x1 = x[..., :half].astype(jnp.float32)
    x2 = x[..., half:].astype(jnp.float32)
    return jnp.concatenate([x1 * cos - x2 * sin, x1 * sin + x2 * cos], axis=-1).astype(x.dtype)

def mla_queries(q_in, q_norm_g, w_q_b, cos, sin):
    b, n, _ = q_in.shape
    q = (rmsnorm(q_in, q_norm_g) @ w_q_b).reshape(b, n, MLA_HEADS, MLA_QK)
    q_nope, q_rope = q[..., :MLA_NOPE], q[..., MLA_NOPE:]
    if cos is not None:
        q_rope = apply_rope_2(q_rope, cos[:, None, :], sin[:, None, :])
    return jnp.concatenate([q_nope, q_rope], axis=-1)

def mla_keys_values(kv_in, kv_norm_g, w_kv_b, cos, sin):
    b, n, _ = kv_in.shape
    c_kv, k_rope = kv_in[..., :MLA_KV_RANK], kv_in[..., MLA_KV_RANK:]
    kv = (rmsnorm(c_kv, kv_norm_g) @ w_kv_b).reshape(b, n, MLA_HEADS, MLA_NOPE + MLA_V)
    k_nope, v = kv[..., :MLA_NOPE], kv[..., MLA_NOPE:]
    if cos is not None:
        k_rope = apply_rope_2(k_rope, cos, sin)
    k_rope = jnp.broadcast_to(k_rope[:, :, None, :], (b, n, MLA_HEADS, MLA_ROPE))
    return jnp.concatenate([k_nope, k_rope], axis=-1), v

def block_attention(q, k, v):
    b, n, h, dk = q.shape
    nb = n // Q_BLOCK
    scale = dk ** -0.5
    q_blocks = q.reshape(b, nb, Q_BLOCK, h, dk).transpose(1, 0, 2, 3, 4)

    def one_block(qb):
        s = jnp.einsum('bqhd,bkhd->bhqk', qb, k, preferred_element_type=jnp.float32) * scale
        p = jax.nn.softmax(s, axis=-1).astype(v.dtype)
        return jnp.einsum('bhqk,bkhd->bqhd', p, v)

    out = lax.map(one_block, q_blocks)
    return out.transpose(1, 0, 2, 3, 4).reshape(b, n, h * v.shape[-1])

def hgrn2_chunk_scan(q, k, v, log_f, s0):
    b, n, h, dk = q.shape
    dv = v.shape[-1]
    nc = n // HG_CHUNK

    def chunks(a):
        return a.reshape(b, nc, HG_CHUNK, h, a.shape[-1]).transpose(1, 0, 3, 2, 4)

    lower_tri = jnp.tril(jnp.ones((HG_CHUNK, HG_CHUNK), dtype=bool))[:, :, None]

    def step(state, inp):
        qc, kc, vc, gc = inp
        cum = jnp.cumsum(gc, axis=2)
        o_inter = jnp.einsum('bhtk,bhkv->bhtv', qc * jnp.exp(cum), state)
        rel = cum[:, :, :, None, :] - cum[:, :, None, :, :]
        decay = jnp.where(lower_tri, jnp.exp(jnp.minimum(rel, 0.0)), 0.0)
        att = jnp.einsum('bhtk,bhtsk,bhsk->bhts', qc, decay, kc)
        o_intra = jnp.einsum('bhts,bhsv->bhtv', att, vc)
        last = cum[:, :, -1:, :]
        state = jnp.exp(last[:, :, 0, :])[..., None] * state + jnp.einsum('bhsk,bhsv->bhkv', kc * jnp.exp(last - cum), vc)
        return state, o_inter + o_intra

    s_final, o = lax.scan(step, s0, (chunks(q), chunks(k), chunks(v), chunks(log_f)))
    return o.transpose(1, 0, 3, 2, 4).reshape(b, n, h, dv), s_final

def hgrn2_gates(z, lb):
    b, n = z.shape[:2]
    f = lb + (1.0 - lb) * jax.nn.sigmoid(z.astype(jnp.float32))
    return (1.0 - f).reshape(b, n, HG_HEADS, HG_DK), jnp.log(f).reshape(b, n, HG_HEADS, HG_DK)

def hgrn2_qv(p):
    b, n = p[2].shape[:2]
    q = (jax.nn.silu(p[2].astype(jnp.float32)) * HG_DK ** -0.5).reshape(b, n, HG_HEADS, HG_DK)
    v = p[5].astype(jnp.float32).reshape(b, n, HG_HEADS, HG_DV)
    return q, v

def hgrn2_readout(o, g, hg_norm_g):
    b, n = g.shape[:2]
    gate = jax.nn.silu(g.astype(jnp.float32)).reshape(b, n, HG_HEADS, HG_DV)
    return (rmsnorm(o, hg_norm_g) * gate).reshape(b, n, HG_WIDTH).astype(g.dtype)

def merge_branches(p, y_mla, y_hg, w_out):
    g_mla = jax.nn.sigmoid(p[7].astype(jnp.float32))
    g_hg = jax.nn.sigmoid(p[8].astype(jnp.float32))
    y = g_mla * y_mla.astype(jnp.float32) + g_hg * y_hg.astype(jnp.float32)
    return y.astype(p[7].dtype) @ w_out

def token_mixer(h_lat, h_ctx, cos, sin, lb_fwd, lb_bwd, w_in, q_norm_g, w_q_b, kv_norm_g, w_kv_b, hg_norm_g, w_out, with_ctx_out):
    lat = split_cols(h_lat @ w_in)
    ctx = split_cols(h_ctx @ w_in)
    k_lat, v_lat = mla_keys_values(lat[1], kv_norm_g, w_kv_b, cos, sin)
    k_ctx, v_ctx = mla_keys_values(ctx[1], kv_norm_g, w_kv_b, None, None)
    q_lat = mla_queries(lat[0], q_norm_g, w_q_b, cos, sin)
    y_mla_lat = block_attention(q_lat, jnp.concatenate([k_lat, k_ctx], axis=1), jnp.concatenate([v_lat, v_ctx], axis=1))
    q_l, v_l = hgrn2_qv(lat)
    q_c, v_c = hgrn2_qv(ctx)
    kf_l, gf_l = hgrn2_gates(lat[3], lb_fwd)
    kb_l, gb_l = hgrn2_gates(lat[4], lb_bwd)
    kf_c, gf_c = hgrn2_gates(ctx[3], lb_fwd)
    kb_c, gb_c = hgrn2_gates(ctx[4], lb_bwd)
    b = h_lat.shape[0]
    s0 = jnp.zeros((b, HG_HEADS, HG_DK, HG_DV), jnp.float32)
    flip = lambda a: jnp.flip(a, axis=1)
    o_cf, s_cf = hgrn2_chunk_scan(q_c, kf_c, v_c, gf_c, s0)
    o_cb, s_cb = hgrn2_chunk_scan(flip(q_c), flip(kb_c), flip(v_c), flip(gb_c), s0)
    o_lf, _ = hgrn2_chunk_scan(q_l, kf_l, v_l, gf_l, s_cf)
    o_lb, _ = hgrn2_chunk_scan(flip(q_l), flip(kb_l), flip(v_l), flip(gb_l), s_cb)
    y_hg_lat = hgrn2_readout(o_lf + flip(o_lb), lat[6], hg_norm_g)
    out_lat = merge_branches(lat, y_mla_lat, y_hg_lat, w_out)
    if not with_ctx_out:
        return out_lat, None
    q_ctx = mla_queries(ctx[0], q_norm_g, w_q_b, None, None)
    y_mla_ctx = block_attention(q_ctx, k_ctx, v_ctx)
    y_hg_ctx = hgrn2_readout(o_cf + flip(o_cb), ctx[6], hg_norm_g)
    return out_lat, merge_branches(ctx, y_mla_ctx, y_hg_ctx, w_out)

def moe_ffn(h, w_router, b_router, w_gate_up, b_gate_up, w_down, b_down):
    shp = h.shape
    t = h.reshape(-1, shp[-1])
    n_tok = t.shape[0]
    n_pair = n_tok * TOP_K
    logits = (t @ w_router + b_router).astype(jnp.float32)
    top_val, top_idx = lax.top_k(logits, TOP_K)
    probs = jax.nn.softmax(top_val, axis=-1)
    flat_e = top_idx.reshape(-1)
    flat_tok = jnp.arange(n_pair, dtype=jnp.int32) // TOP_K
    order = jnp.argsort(flat_e)
    sorted_e = flat_e[order]
    counts = jnp.bincount(flat_e, length=N_EXPERTS)
    padded = (counts + MOE_BLOCK - 1) // MOE_BLOCK * MOE_BLOCK
    start = jnp.cumsum(counts) - counts
    pad_end = jnp.cumsum(padded)
    pad_start = pad_end - padded
    dest_sorted = pad_start[sorted_e] + jnp.arange(n_pair, dtype=jnp.int32) - start[sorted_e]
    dest = jnp.zeros((n_pair,), jnp.int32).at[order].set(dest_sorted.astype(jnp.int32))
    n_rows = n_pair + N_EXPERTS * MOE_BLOCK
    n_blocks = n_rows // MOE_BLOCK
    row_tok = jnp.full((n_rows,), n_tok, jnp.int32).at[dest].set(flat_tok)
    t_ext = jnp.concatenate([t, jnp.zeros((1, t.shape[-1]), t.dtype)], axis=0)
    x_rows = t_ext[row_tok].reshape(n_blocks, MOE_BLOCK, -1)
    block_start = jnp.arange(n_blocks, dtype=jnp.int32) * MOE_BLOCK
    block_e = jnp.minimum(jnp.searchsorted(pad_end, block_start, side='right'), N_EXPERTS - 1)

    def expert_block(args):
        xb, e = args
        gu = xb @ w_gate_up[e] + b_gate_up[e]
        x_glu = jnp.minimum(gu[:, 0::2], SWIGLU_LIMIT)
        x_lin = jnp.clip(gu[:, 1::2], -SWIGLU_LIMIT, SWIGLU_LIMIT)
        act = x_glu * jax.nn.sigmoid(SWIGLU_ALPHA * x_glu) * (x_lin + 1)
        return act @ w_down[e] + b_down[e]

    y_rows = lax.map(expert_block, (x_rows, block_e)).reshape(n_rows, -1)
    y_pairs = y_rows[dest].reshape(n_tok, TOP_K, -1)
    out = jnp.einsum('tk,tkd->td', probs.astype(y_pairs.dtype), y_pairs)
    return out.reshape(shp)

def second_inputs(seed: int = 0) -> dict:
    key = jax.random.key(seed)
    ks = jax.random.split(key, 24)
    f32 = jnp.float32
    nrm = lambda k, shape, scale: jax.random.normal(k, shape, f32) * scale
    gain = lambda k, shape: 1.0 + 0.02 * jax.random.normal(k, shape, f32)
    return {
        'x': nrm(ks[0], (BATCH, SEQ, D_MODEL), 1.0),
        'c': nrm(ks[1], (BATCH, D_MODEL), 1.0),
        'ctx': nrm(ks[2], (BATCH, CTX_LEN, D_MODEL), 1.0),
        'c_ctx': nrm(ks[3], (D_MODEL,), 1.0),
        'w_mod': nrm(ks[4], (DEPTH, D_MODEL, N_MOD * D_MODEL), 0.5 * D_MODEL ** -0.5),
        'b_mod': nrm(ks[5], (DEPTH, N_MOD * D_MODEL), 0.02),
        'norm_mix_g': gain(ks[6], (DEPTH, D_MODEL)),
        'w_in': nrm(ks[7], (DEPTH, D_MODEL, D_IN), D_MODEL ** -0.5),
        'mla_q_norm_g': gain(ks[8], (DEPTH, MLA_Q_RANK)),
        'w_q_b': nrm(ks[9], (DEPTH, MLA_Q_RANK, MLA_HEADS * MLA_QK), MLA_Q_RANK ** -0.5),
        'mla_kv_norm_g': gain(ks[10], (DEPTH, MLA_KV_RANK)),
        'w_kv_b': nrm(ks[11], (DEPTH, MLA_KV_RANK, MLA_HEADS * (MLA_NOPE + MLA_V)), MLA_KV_RANK ** -0.5),
        'hg_lb_logits': nrm(ks[12], (2, DEPTH + 1, HG_FDIM), 1.0),
        'hg_norm_g': gain(ks[13], (DEPTH, HG_DV)),
        'w_out': nrm(ks[14], (DEPTH, D_MODEL, D_MODEL), D_MODEL ** -0.5),
        'norm_ffn_g': gain(ks[15], (DEPTH, D_MODEL)),
        'w_router': nrm(ks[16], (DEPTH, D_MODEL, N_EXPERTS), D_MODEL ** -0.5),
        'b_router': nrm(ks[17], (DEPTH, N_EXPERTS), 0.01),
        'w_gate_up': nrm(ks[18], (DEPTH, N_EXPERTS, D_MODEL, 2 * D_EXPERT), D_MODEL ** -0.5),
        'b_gate_up': nrm(ks[19], (DEPTH, N_EXPERTS, 2 * D_EXPERT), 0.01),
        'w_down': nrm(ks[20], (DEPTH, N_EXPERTS, D_EXPERT, D_MODEL), D_EXPERT ** -0.5),
        'b_down': nrm(ks[21], (DEPTH, N_EXPERTS, D_MODEL), 0.01),
        'final_norm_g': gain(ks[22], (D_MODEL,)),
    }

def second_block(x, c, ctx, c_ctx, w_mod, b_mod, norm_mix_g, w_in, mla_q_norm_g, w_q_b, mla_kv_norm_g, w_kv_b, hg_lb_logits, hg_norm_g, w_out, norm_ffn_g, w_router, b_router, w_gate_up, b_gate_up, w_down, b_down, final_norm_g):
    rows = x.shape[1] // GRID_W
    cos, sin = axial_rope_tables(rows)
    lb = jnp.cumsum(jax.nn.softmax(hg_lb_logits.astype(jnp.float32), axis=1), axis=1)
    silu_c = jax.nn.silu(c)
    silu_cc = jax.nn.silu(c_ctx)
    n_ctx = ctx.shape[1]
    for l in range(DEPTH):
        last = l == DEPTH - 1
        mod_lat = jnp.split((silu_c @ w_mod[l] + b_mod[l])[:, None, :], N_MOD, axis=-1)
        mod_ctx = jnp.split((silu_cc @ w_mod[l] + b_mod[l])[None, None, :], N_MOD, axis=-1)
        h_lat = rmsnorm(x, norm_mix_g[l]) * (1 + mod_lat[1]) + mod_lat[0]
        h_ctx = rmsnorm(ctx, norm_mix_g[l]) * (1 + mod_ctx[1]) + mod_ctx[0]
        mix_lat, mix_ctx = token_mixer(h_lat, h_ctx, cos, sin, lb[0, l], lb[1, l], w_in[l], mla_q_norm_g[l], w_q_b[l], mla_kv_norm_g[l], w_kv_b[l], hg_norm_g[l], w_out[l], not last)
        x = x + mod_lat[2] * mix_lat
        h_lat = rmsnorm(x, norm_ffn_g[l]) * (1 + mod_lat[4]) + mod_lat[3]
        if last:
            x = x + mod_lat[5] * moe_ffn(h_lat, w_router[l], b_router[l], w_gate_up[l], b_gate_up[l], w_down[l], b_down[l])
        else:
            ctx = ctx + mod_ctx[2] * mix_ctx
            h_ctx = rmsnorm(ctx, norm_ffn_g[l]) * (1 + mod_ctx[4]) + mod_ctx[3]
            y = moe_ffn(jnp.concatenate([h_ctx, h_lat], axis=1), w_router[l], b_router[l], w_gate_up[l], b_gate_up[l], w_down[l], b_down[l])
            ctx = ctx + mod_ctx[5] * y[:, :n_ctx]
            x = x + mod_lat[5] * y[:, n_ctx:]
    return rmsnorm(x, final_norm_g)


def setup_inputs(seed=0):
    out = dict(first_inputs(seed))
    for name, value in second_inputs(seed + 1).items():
        if name != "x":
            out[name + "_2"] = value
    return out


def reference(
    x, mem, positions, g_pre_mix, g_mem, w_in, w_mem_kv, conv_w, g_attn_out, g_conv_out,
    g_xattn_out, w_out, g_post_mix, g_pre_mlp, w_up, w_down, g_post_mlp, c_2, ctx_2, c_ctx_2,
    w_mod_2, b_mod_2, norm_mix_g_2, w_in_2, mla_q_norm_g_2, w_q_b_2, mla_kv_norm_g_2, w_kv_b_2,
    hg_lb_logits_2, hg_norm_g_2, w_out_2, norm_ffn_g_2, w_router_2, b_router_2, w_gate_up_2,
    b_gate_up_2, w_down_2, b_down_2, final_norm_g_2,
):
    x = first_block(
        x, mem, positions, g_pre_mix, g_mem, w_in, w_mem_kv, conv_w, g_attn_out, g_conv_out,
        g_xattn_out, w_out, g_post_mix, g_pre_mlp, w_up, w_down, g_post_mlp,
    )
    return second_block(
        x, c_2, ctx_2, c_ctx_2, w_mod_2, b_mod_2, norm_mix_g_2, w_in_2, mla_q_norm_g_2, w_q_b_2,
        mla_kv_norm_g_2, w_kv_b_2, hg_lb_logits_2, hg_norm_g_2, w_out_2, norm_ffn_g_2,
        w_router_2, b_router_2, w_gate_up_2, b_gate_up_2, w_down_2, b_down_2, final_norm_g_2,
    )


_drawn_inputs = setup_inputs


def setup_inputs(seed=0):
    import zlib

    import numpy as np

    out = dict(_drawn_inputs(seed))
    spreads = {}
    factors = {'g_conv_out': 2.922,
     'g_xattn_out': 2.709,
     'ctx_2': 8.0,
     'c_ctx_2': 5.487,
     'b_mod_2': 4.014,
     'norm_mix_g_2': 8.0,
     'mla_q_norm_g_2': 8.0,
     'w_q_b_2': 5.348,
     'mla_kv_norm_g_2': 8.0,
     'hg_lb_logits_2': 8.0,
     'hg_norm_g_2': 8.0,
     'norm_ffn_g_2': 6.242,
     'b_router_2': 35.258,
     'b_gate_up_2': 55.432,
     'b_down_2': 200.0,
     'final_norm_g_2': 26.611}
    for name, (base, spread) in spreads.items():
        noise = np.random.default_rng([zlib.crc32(name.encode()), seed]).standard_normal(out[name].shape)
        drawn = base * np.exp(spread * noise) if base else spread * noise
        out[name] = jnp.asarray(drawn.astype(out[name].dtype))
    for name, factor in factors.items():
        out[name] = (out[name] * factor).astype(out[name].dtype)
    return out
```

```python
import numpy as np
import concourse.bass as bass
from concourse import mybir
from contextlib import ExitStack

P = 128
D = 1024
DC = D // P
T = 512
TT = T // P
M = 256
TA = T + M
AC = TA // P
DFF = 4096
HEADS1, DH1 = 8, 64
EPS = 1e-6
NEG = -1e30
SLOT = 2048
RING = 5
N_EXP, TOPK = 32, 4
N_BLOCKS = T * TOPK // P + N_EXP
N_ROWS = (N_BLOCKS + 1) * P
MT = 24
MC = 1024
LEVELS = 7

C_Q, C_KV, C_KR, C_HQ, C_ZF, C_ZB, C_V, C_G, C_P7, C_P8 = 0, 768, 1024, 1088, 2112, 3136, 4160, 5184, 6208, 7232

VECS = [("g_pre_mix", 8), ("g_mem", 8), ("conv_w", 6), ("g_attn_out", 4), ("g_conv_out", 2), ("g_xattn_out", 2),
        ("g_post_mix", 8), ("g_pre_mlp", 8), ("g_post_mlp", 8), ("c_2", 8), ("c_ctx_2", 8), ("b_mod_2", 48),
        ("norm_mix_g_2", 8), ("mla_q_norm_g_2", 6), ("mla_kv_norm_g_2", 2), ("hg_lb_logits_2", 32),
        ("hg_norm_g_2", 1), ("norm_ffn_g_2", 8), ("final_norm_g_2", 8)]
VEC_AT = {}
_n = 0
for _name, _k in VECS:
    VEC_AT[_name] = _n
    _n += _k
N_VEC = _n

CONSTS = [("ident", P), ("ones", P), ("rot", P), ("band", T), ("levels", 15 * P // 4), ("reset", TA),
          ("inv_freq", 1), ("rot_sign", 1), ("axial_cos", T), ("axial_sin", T), ("tri", P), ("expert_no", N_EXP),
          ("block_no", N_BLOCKS), ("token_no", TT)]
CONST_AT = {}
_n = 0
for _name, _k in CONSTS:
    CONST_AT[_name] = _n
    _n += _k
N_CONST = _n


def weight_tiles():
    out = []

    def cols(name, at, n, kc=DC, k0=0):
        out.append((name, k0, kc, at, n))

    for i in range(10):
        cols("w_in", 256 * i, 256)
    for i in range(2):
        cols("w_mem_kv", 256 * i, 256)
    for i in range(4):
        cols("w_out", 256 * i, 256)
    for i in range(16):
        cols("w_up", 256 * i, 256)
    for i in range(4):
        for k in range(4):
            cols("w_down", 256 * i, 256, DC, DC * k)
    for i in range(24):
        cols("w_mod_2", 256 * i, 256)
    for i in range(4):
        cols("w_in_2", 256 * i, 256)
    cols("w_in_2", C_KR, 64)
    for g in range(4):
        cols("w_q_b_2", 384 * g, 192, 6)
        cols("w_q_b_2", 384 * g + 192, 192, 6)
        cols("w_kv_b_2", 512 * g, 512, 2)
    for g in range(4):
        for at in (C_HQ, C_ZF, C_ZB, C_V, C_G, C_P7, C_P8):
            cols("w_in_2", at + 256 * g, 256)
    for i in range(4):
        cols("w_out_2", 256 * i, 256)
    return out


WT = weight_tiles()
NT = len(WT)


def build(nc, wt, xT, memT, ctxT, pos, vecs, consts, wr, br, wgu, bgu, wdn, bdn, out, hrows, tokof, yrows, blk_dram, dbg=None, stop=None):
    fp32, i32, u8 = mybir.dt.float32, mybir.dt.int32, mybir.dt.uint8
    ALU, ACT, AX = mybir.AluOpType, mybir.ActivationFunctionType, mybir.AxisListType
    F = ACT

    ctx = ExitStack()
    with ctx:
        def sb(name, cols, dt=fp32):
            return ctx.enter_context(nc.sbuf_tensor(name, [P, cols], dt))

        def sem(name):
            return ctx.enter_context(nc.semaphore(name))

        def v3(ap, n):
            return ap.rearrange("p (a b) -> p a b", a=n)

        ring = sb("ring", RING * SLOT)
        x = v3(sb("x", DC * T)[:, :], DC)
        cst = sb("cst", N_CONST)
        vec = sb("vec", N_VEC)
        sq = v3(sb("sq", 2 * T)[:, :], 2)
        ms = sb("ms", T)
        rstd = sb("rstd", T)
        mod = sb("mod", 96)
        small = sb("small", 160)
        zeros = sb("zeros", 512)[:, :]
        arena = sb("arena", 32000)
        G = ctx.enter_context(nc.psum_tensor("product_banks", [P, 2048], fp32))
        jb = [G[:, 512 * i:512 * i + 512] for i in range(4)]
        S = ctx.enter_context(nc.psum_tensor("score_banks", [P, 1024], fp32))
        PT = ctx.enter_context(nc.psum_tensor("turn_bank", [P, 512], fp32))
        PO = ctx.enter_context(nc.psum_tensor("out_bank", [P, 512], fp32))
        LB = [S[:, 0:512], S[:, 512:1024]]

        def const(name):
            k = dict(CONSTS)[name]
            return cst[:, CONST_AT[name]:CONST_AT[name] + k]

        def vcol(name, i=0, n=1):
            return vec[:, VEC_AT[name] + i:VEC_AT[name] + i + n]

        ident, ones, rot = const("ident"), const("ones"), const("rot")
        level_masks = v3(const("levels").bitcast(u8), 15)

        class Area:
            def __init__(self, at=0):
                self.at = at

            def take(self, cols, n=None):
                a = arena[:, self.at:self.at + cols]
                self.at += cols
                assert self.at <= 32000, self.at
                return v3(a, n) if n else a

        A = Area()
        h = A.take(DC * T, DC)
        mark_h = A.at
        q1 = A.take(4 * T, 4)
        k1 = A.take(4 * T, 4)
        v1 = A.take(TT * 512, TT)
        cb, cc, cu = A.take(2 * T, 2), A.take(2 * T, 2), A.take(2 * T, 2)
        qx = A.take(2 * T, 2)
        mem = A.take(DC * M, DC)
        hm = A.take(DC * M, DC)
        km = A.take(2 * M, 2)
        vm = A.take(2 * M, 2)
        cosT, sinT, ang, trn = A.take(T), A.take(T), A.take(T), A.take(T)
        probs1, probsT1, masked = A.take(2 * TA, 2), A.take(TA), A.take(T)
        yconv = A.take(2 * T, 2)
        yatt = mem.rearrange("p a b -> p (a b)")
        yatt = v3(yatt[:, 0:4 * T], 4)
        yxa = v3(hm.rearrange("p a b -> p (a b)")[:, 0:2 * T], 2)
        A = Area(mark_h)
        mix_out = A.take(DC * T, DC)
        ffn = A.take(DFF // P * T, DFF // P)
        A = Area()
        ha = A.take(DC * TA, DC)
        ymla = A.take(DC * T, DC)
        mark2 = A.at
        cx = A.take(DC * M, DC)
        cs = A.take(16)
        A = Area(mark2)
        qin = A.take(6 * T, 6)
        ckv = A.take(2 * TA, 2)
        kr = A.take(TA)
        qn = A.take(2 * T, 2)
        qr = A.take(2 * T, 2)
        kn = A.take(2 * TA, 2)
        vv = A.take(AC * 256, AC)
        probs2, probsT2 = A.take(2 * TA, 2), A.take(TA)
        tmp2 = A.take(T)
        A = Area(mark2)
        hq = A.take(2 * T, 2)
        hg = A.take(2 * T, 2)
        s7 = A.take(2 * T, 2)
        s8 = A.take(2 * T, 2)
        zs = A.take(4 * TA, 4)
        hv = A.take(AC * 256, AC)
        lnA = A.take(TA)
        kk = A.take(2 * TA, 2)
        cum = A.take(2 * TA, 2)
        qq = A.take(T)
        dlt = A.take(2 * TA, 2)
        E = A.take(2 * TA, 2)
        X = A.take(2 * T, 2)
        qe = A.take(2 * T, 2)
        kT = A.take(TA, AC)
        St = A.take(2 * 5 * P, 10)
        At = A.take(T)
        osb = A.take(T)
        el = A.take(12, 2)
        A = Area(mark2)
        mout2 = A.take(DC * T, DC)

        mw = arena[:, 0:MT * MC].rearrange("p (a b) -> p a b", a=MT)
        A = Area(MT * MC)
        aT = A.take(1024, 8)
        brow = A.take(3072)
        lg = A.take(TT * N_EXP, TT)
        top8 = A.take(TT * 8, TT)
        idx8 = A.take(TT * 8, TT)
        idxf = A.take(TT * 4, TT)
        hot = A.take(TT * 4 * N_EXP)
        hot2 = A.take(TT * 4 * N_EXP)
        member = A.take(TT * N_EXP, TT)
        cmpb = arena[:, 0:N_BLOCKS * N_EXP]
        blocks_of = A.take(N_EXP)
        block_end = A.take(N_EXP)
        first_row = A.take(N_EXP)
        rank = A.take(TT * N_EXP, TT)
        destf = A.take(16)
        desti = A.take(16)
        prob = A.take(16)
        tokno = A.take(TT)
        tab = A.take(N_BLOCKS + 16)
        block_expert = A.take(N_BLOCKS)
        wrs = A.take(DC * N_EXP, DC)
        brs = A.take(N_EXP)
        idx_in = A.take(1)
        held = A.take(1)
        rg = ring[:, :]
        h3 = v3(rg[:, 0:4096], DC)
        hr = v3(rg[:, 4096:8192], TT)
        biasb = rg[:, 0:3072]
        tbuf = rg[:, 3072:4096]
        glu = rg[:, 4096:4608]
        lin = rg[:, 4608:5120]
        sig = rg[:, 5120:5632]
        actb = rg[:, 5632:6656]
        yb = rg[:, 6656:7680]
        xg = rg[:, 7680:8704]
        xTb = v3(rg[:, 8704:9728], 8)
        acc = arena[:, 0:4096].rearrange("p (a b) -> p a b", a=TT)
        yg = arena[:, 4096:6144].rearrange("p (a b) -> p a b", a=2)
        yT = arena[:, 6144:10240].rearrange("p (a b) -> p a b", a=DC)
        fin = arena[:, 10240:14336].rearrange("p (a b) -> p a b", a=DC)

        s_const = sem("constants_loaded")
        s_in = sem("activations_loaded")
        s_pos = sem("positions_loaded")
        s_tok = sem("side_tokens_loaded")
        s_slot = [sem(f"weights_loaded{i}") for i in range(RING)]
        s_pair = sem("pair_ready")
        s_evac = sem("pair_evacuated")
        s_sq = sem("squares_ready")
        s_mm = sem("squares_summed")
        s_ms = sem("mean_squares_ready")
        s_rt = sem("roots_ready")
        s_norm = sem("norm_written")
        s_rot_in = sem("rope_input_ready")
        s_rot = sem("rope_turned")
        s_rope = sem("rope_written")
        s_sc = sem("scores_ready")
        s_max = sem("max_ready")
        s_exp = sem("exps_ready")
        s_prob = sem("probs_ready")
        s_tr = sem("probs_turned")
        s_trc = sem("turned_copied")
        s_pv = sem("values_summed")
        s_out = sem("heads_written")
        s_vec = sem("vector_step")
        s_act = sem("scalar_step")
        s_ang = sem("angles_ready")
        s_sin = sem("sines_ready")
        s_ffn = sem("ffn_squared")
        s_silu = sem("conditions_ready")
        s_silc = sem("conditions_exp")
        s_res = sem("residual_ready")
        s_modr = sem("modulation_ready")
        s_lb = sem("bounds_max_ready")
        s_lbe = sem("bounds_exp_ready")
        s_f = sem("forget_clamped")
        s_ln = sem("forget_logged")
        s_cum = sem("decay_summed")
        s_ec = sem("decay_exps")
        s_kd = sem("keys_decayed")
        s_kt = sem("keys_turned")
        s_ktc = sem("turned_keys_copied")
        s_ds = sem("state_terms")
        s_st = sem("states_ready")
        s_d = sem("level_difference")
        s_e = sem("level_exps")
        s_x = sem("level_operand")
        s_p = sem("level_products")
        s_at = sem("weights_gathered")
        s_o = sem("outputs_summed")
        s_osb = sem("outputs_copied")
        s_hg = sem("head_merged")
        s_sil = sem("silu_factor")
        s_end = sem("output_stored")
        s_route_w = sem("router_weights_loaded")
        s_zero = sem("zeros_ready")
        s_held = sem("waits_held")
        s_yclear = sem("row_tables_cleared")
        s_lgp = sem("logit_products")
        s_top = sem("top_maxima")
        s_tope = sem("top_exps")
        s_mem = sem("membership_ready")
        s_rank = sem("ranks_ready")
        s_dest = sem("rows_assigned")
        s_tab = sem("block_table_ready")
        s_hT = sem("h_rows_turned")
        s_hc = sem("h_rows_copied")
        s_hst = sem("h_rows_stored")
        s_scat = sem("row_tokens_scattered")
        s_w = [sem(f"expert_tile_loaded{i}") for i in range(MT)]
        s_used = sem("expert_tiles_used")
        s_brow = sem("bias_rows_loaded")
        s_bb = sem("bias_broadcast")
        s_tk = sem("block_tokens_loaded")
        s_ga = sem("block_inputs_gathered")
        s_xtp = sem("inputs_turned")
        s_xtc = sem("turned_inputs_copied")
        s_glu = sem("glu_ready")
        s_sig = sem("sigmoid_ready")
        s_lg = sem("gated_linear_ready")
        s_actr = sem("activation_ready")
        s_atp = sem("activation_turned")
        s_atc = sem("turned_activation_copied")
        s_y = sem("expert_rows_ready")
        s_yst = sem("expert_rows_stored")
        s_vl = sem("vector_loop_step")
        s_yg = [sem(f"token_rows_gathered{i}") for i in range(2)]
        s_acc = sem("token_sum_ready")
        s_tT = sem("token_sums_turned")
        s_tTc = sem("turned_sums_copied")

        def tile_ap(t):
            _, _, kc, _, n = WT[t]
            s = t % RING
            return v3(ring[:, s * SLOT:s * SLOT + kc * n], kc)

        pairs = []
        stages = {}
        state = {"tile": 0}

        def next_tile():
            state["tile"] += 1
            return state["tile"] - 1

        def pair(stage, groups, evacs):
            pairs.append((groups, evacs))
            stages.setdefault(stage, [len(pairs) - 1, len(pairs)])[1] = len(pairs)

        def feature_pair(stage, tiles, src, width, dst, func=F.Copy, scale=1.0, bias=None, rows=(P, P)):
            groups, evacs = [], []
            at = 0
            for m in range(len(dst)):
                mm = []
                for t in tiles:
                    w = tile_ap(t)
                    k0 = WT[t][1]
                    for k in range(WT[t][2]):
                        mm.append((t, w[:, k, at:at + rows[m]], src[:, (k0 + k), 0:width] if width else src[:, k0 + k, :]))
                groups.append((mm, rows[m], width))
                evacs.append((dst[m], func, scale, bias[m] if bias else 0.0, rows[m], width))
                at += rows[m]
            pair(stage, groups, evacs)

        def token_pair(stage, t, src, tiles, wcols, n, dst):
            groups, evacs = [], []
            for i, j in enumerate(tiles):
                w = tile_ap(t)
                mm = [(t, src[:, k, P * j:P * j + P], wcols(w, k)) for k in range(WT[t][2])]
                groups.append((mm, P, n))
                evacs.append((dst[i], F.Copy, 1.0, 0.0, P, n))
            pair(stage, groups, evacs)

        plain = lambda w, k: w[:, k, :]
        for i in range(10):
            t = next_tile()
            if i < 4:
                to = q1 if i < 2 else k1
                feature_pair("in1", [t], h, T, [to[:, 2 * (i % 2), :], to[:, 2 * (i % 2) + 1, :]])
            elif i < 6:
                for j in (0, 2):
                    token_pair("in1", t, h, [j, j + 1], plain, 256,
                               [v1[:, j, 256 * (i - 4):256 * (i - 3)], v1[:, j + 1, 256 * (i - 4):256 * (i - 3)]])
            else:
                to = (cb, cc, cu, qx)[i - 6]
                feature_pair("in1", [t], h, T, [to[:, 0, :], to[:, 1, :]])
        feature_pair("mem", [next_tile()], hm, M, [km[:, 0, :], km[:, 1, :]])
        token_pair("mem", next_tile(), hm, [0, 1], plain, 256, [vm[:, 0, :], vm[:, 1, :]])
        for i in range(4):
            feature_pair("out1", [next_tile()], h, T, [mix_out[:, 2 * i + m, :] for m in range(2)])
        for i in range(16):
            feature_pair("up", [next_tile()], h, T, [ffn[:, 2 * i + m, :] for m in range(2)], F.Relu)
        for i in range(4):
            feature_pair("down", [next_tile() for _ in range(4)], ffn, T, [mix_out[:, 2 * i + m, :] for m in range(2)])
        modv = v3(mod[:, :], 48)
        for i in range(24):
            feature_pair("mod", [next_tile()], v3(cs, 8), 2, [modv[:, 2 * i + m, :] for m in range(2)],
                         F.Identity, 1.0, [vcol("b_mod_2", 2 * i + m) for m in range(2)])
        hctx = ha[:, :, T:TA]
        for i in range(3):
            feature_pair("in2", [next_tile()], ha, T, [qin[:, 2 * i + m, :] for m in range(2)])
        t = next_tile()
        feature_pair("in2", [t], ha, T, [ckv[:, m, 0:T] for m in range(2)])
        feature_pair("in2", [t], hctx, M, [ckv[:, m, T:TA] for m in range(2)])
        t = next_tile()
        feature_pair("in2", [t], ha, T, [kr[0:64, 0:T]], rows=(64,))
        feature_pair("in2", [t], hctx, M, [kr[0:64, T:TA]], rows=(64,))
        for g in range(4):
            for m in range(2):
                feature_pair(f"mla{g}", [next_tile()], qin, T, [qn[:, m, :], qr[0:64, m, :]], rows=(P, 64))
            t = next_tile()
            w = tile_ap(t)
            for a, b in ((0, T), (T, TA)):
                groups = [([(t, w[:, k, 256 * m:256 * m + P], ckv[:, k, a:b]) for k in range(2)], P, b - a) for m in range(2)]
                pair(f"mla{g}", groups, [(kn[:, m, a:b], F.Copy, 1.0, 0.0, P, b - a) for m in range(2)])
            vcols = lambda w, k: w[:, k, :].rearrange("p (h c) -> p h c", h=2)[:, :, P:2 * P]
            for j in range(0, AC, 2):
                token_pair(f"mla{g}", t, ckv, [j, j + 1], vcols, 256, [vv[:, j, :], vv[:, j + 1, :]])
        for g in range(4):
            st = f"hg{g}"
            feature_pair(st, [next_tile()], ha, T, [hq[:, m, :] for m in range(2)])
            for d in range(2):
                t = next_tile()
                feature_pair(st, [t], ha, T, [zs[:, 2 * d + m, 0:T] for m in range(2)], F.Sigmoid)
                feature_pair(st, [t], hctx, M, [zs[:, 2 * d + m, T:TA] for m in range(2)], F.Sigmoid)
            t = next_tile()
            for j in range(0, AC, 2):
                token_pair(st, t, ha, [j, j + 1], plain, 256, [hv[:, j, :], hv[:, j + 1, :]])
            feature_pair(st, [next_tile()], ha, T, [hg[:, m, :] for m in range(2)])
            feature_pair(st, [next_tile()], ha, T, [s7[:, m, :] for m in range(2)], F.Sigmoid)
            feature_pair(st, [next_tile()], ha, T, [s8[:, m, :] for m in range(2)], F.Sigmoid)
        for i in range(4):
            feature_pair("out2", [next_tile()], ymla, T, [mout2[:, 2 * i + m, :] for m in range(2)])
        assert state["tile"] == NT
        last_pair_of = {}
        for n, (groups, _) in enumerate(pairs):
            for mm, _, _ in groups:
                for t, _, _ in mm:
                    last_pair_of[t] = n

        NORMS = [("pre_mix", x, 8, T), ("mem", mem, 8, M), ("attn", yatt, 4, T), ("conv", yconv, 2, T),
                 ("xattn", yxa, 2, T), ("post_mix", mix_out, 8, T), ("pre_mlp", x, 8, T), ("post_mlp", mix_out, 8, T),
                 ("mix2", x, 8, T), ("ctx", cx, 8, M), ("qin", qin, 6, T), ("ckv_lat", ckv, 2, T),
                 ("ckv_ctx", ckv[:, :, T:TA], 2, M)]
        NORMS += [(f"head{n}", osb.unsqueeze(1), 1, T) for n in range(8)]
        NORMS += [("ffn2", x, 8, T), ("final", x, 8, T)]
        NI = {n[0]: i for i, n in enumerate(NORMS)}
        chunk0 = [sum(n[2] for n in NORMS[:i]) for i in range(len(NORMS))]

        UNITS = []
        for hd in range(HEADS1):
            r = slice(64 * (hd % 2), 64 * (hd % 2) + 64)
            for i in range(TT):
                nk = P * (i + 1)
                UNITS.append(dict(sc=[[(q1[r, hd // 2, P * i:P * i + P], k1[r, hd // 2, 0:nk], 0, nk)]], nk=nk,
                                  v=[v1[:, j, P * (hd // 2):P * (hd // 2) + P] for j in range(i + 1)], rows=r,
                                  dst=yatt[r, hd // 2, P * i:P * i + P], scale=DH1 ** -0.5,
                                  mask=const("band")[:, T - P - P * i:T - P - P * i + nk], pr=probs1, pt=probsT1))
        U_X = len(UNITS)
        for hd in range(4):
            r = slice(64 * (hd % 2), 64 * (hd % 2) + 64)
            for i in range(TT):
                UNITS.append(dict(sc=[[(qx[r, hd // 2, P * i:P * i + P], km[r, hd // 2, :], 0, M)]], nk=M,
                                  v=[vm[:, j, P * (hd // 2):P * (hd // 2) + P] for j in range(2)], rows=r,
                                  dst=yxa[r, hd // 2, P * i:P * i + P], scale=64 ** -0.5, mask=None, pr=probs1, pt=probsT1))
        U_M = len(UNITS)
        for hd in range(8):
            m = hd % 2
            for i in range(TT):
                qs = slice(P * i, P * i + P)
                UNITS.append(dict(sc=[[(qn[:, m, qs], kn[:, m, a:b], a, b), (qr[0:64, m, qs], kr[0:64, a:b], a, b)]
                                      for a, b in ((0, T), (T, TA))], nk=TA,
                                  v=[vv[:, j, P * m:P * m + P] for j in range(AC)], rows=slice(0, P),
                                  dst=ymla[:, hd, qs], scale=192 ** -0.5, mask=None, pr=probs2, pt=probsT2))
        turns0 = []
        n = 0
        for u in UNITS:
            turns0.append(n)
            n += (len(u["v"]) + 3) // 4
        ROPES = [(q1[:, c, :], cosT, sinT, P) for c in range(4)] + [(k1[:, c, :], cosT, sinT, P) for c in range(4)]
        ac_, as_ = const("axial_cos"), const("axial_sin")
        ROPES += [(kr[0:64, 0:T], ac_[0:64, :], as_[0:64, :], 64)]
        for g in range(4):
            ROPES += [(qr[0:64, m, :], ac_[0:64, :], as_[0:64, :], 64) for m in range(2)]

        level_half = [P >> (i + 1) for i in range(LEVELS)]
        SEQ = [[4, 5, 0, 1, 2, 3], [5, 4, 3, 2, 1, 0]]

        tab_i = tab.bitcast(i32)
        desti_u = desti.bitcast(mybir.dt.uint32)
        NORM_FINAL = 13
        block = ctx.enter_context(nc.Block())

        @block.sync
        def _(sp):
            sp.dma_start(cst[:, :], consts).then_inc(s_const, 16)
            sp.dma_start(vec[:, :], vecs).then_inc(s_const, 16)
            sp.dma_start(x, xT).then_inc(s_in, 16)
            for t in range(NT if stop != "x1" else 48):
                if t >= RING:
                    sp.wait_ge(s_pair, last_pair_of[t - RING] + 1)
                _, _, kc, _, n = WT[t]
                s = t % RING
                sp.dma_start(ring[:, s * SLOT:s * SLOT + kc * n], wt[t, :, 0:kc * n]).then_inc(s_slot[s], 16)
            if dbg is None:
                sp.wait_ge(s_hg, 8)
                sp.dma_start(wrs, wr).then_inc(s_route_w, 16)
                sp.dma_start(brs[0:1, :], br).then_inc(s_route_w, 16)
                for i in range(TT):
                    sp.wait_ge(s_hc, i + 1)
                    sp.dma_start(hrows[P * i:P * i + P, :], hr[:, i, :]).then_inc(s_hst, 16)
                sp.wait_ge(s_tab, 1)
                nb = sp.value_load(tab_i[0:1, N_BLOCKS:N_BLOCKS + 1], min_val=T * TOPK // P, max_val=N_BLOCKS)

                def load_expert(e, b):
                    if b is not None:
                        sp.wait_ge(s_bb, b)
                    sp.dma_start(brow[0:1, 0:2048], bgu[bass.ds(e, 1), :]).then_inc(s_brow, 16)
                    sp.dma_start(brow[0:1, 2048:3072], bdn[bass.ds(e, 1), :]).then_inc(s_brow, 16)
                    for t in range(MT):
                        if b is not None:
                            sp.wait_ge(s_used, b * MT + (t + 1 - MT))
                        if t < 16:
                            k, hf = t % 8, t // 8
                            src = wgu[bass.ds(e, 1), P * k:P * k + P, MC * hf:MC * hf + MC]
                        else:
                            k = t - 16
                            src = wdn[bass.ds(e, 1), P * k:P * k + P, :]
                        sp.dma_start(mw[:, t, :], src.rearrange("a p n -> (a p) n")).then_inc(s_w[t], 16)

                load_expert(sp.value_load(tab_i[0:1, 0:1], min_val=0, max_val=N_EXP - 1), None)
                with sp.Fori(1, nb) as b:
                    load_expert(sp.value_load(tab_i[0:1, bass.ds(b, 1)], min_val=0, max_val=N_EXP - 1), b)
                sp.wait_ge(s_norm, NORM_FINAL)
                sp.dma_start(out, fin).then_inc(s_end, 16)
                sp.wait_ge(s_end, 16)
            if dbg is not None:
                sp.wait_ge(s_hg if stop == "hg" else s_res, 1 if stop == "x1" else 8 if stop == "hg" else 2)
                src = x if stop != "hg" else ymla
                sp.dma_start(dbg, src).then_inc(s_end, 16)
                sp.wait_ge(s_end, 16)

        @block.gpsimd
        def _(gp):
            gp.dma_start(ang.bitcast(i32), pos.partition_broadcast(P)).then_inc(s_pos, 16)
            gp.dma_start(mem, memT).then_inc(s_tok, 16)
            gp.memset(zeros, 0.0).then_inc(s_zero, 1)
            gp.wait_ge(s_zero, 1)
            gp.dma_start(tokof.rearrange("(p n) o -> p (n o)", p=P),
                         zeros.bitcast(i32)[:, 0:N_ROWS // P]).then_inc(s_yclear, 16)
            gp.wait_ge(s_res, 1)
            gp.dma_start(cx, ctxT).then_inc(s_tok, 16)
            if dbg is not None:
                return
            gp.wait_ge(s_hg, 8)
            gp.wait_ge(s_yclear, 16)
            gp.wait_ge(s_dest, 1)
            for i in range(TT):
                for k in range(TOPK):
                    j = TOPK * i + k
                    gp.indirect_dma_start(tokof, bass.IndirectOffsetOnAxis(desti_u[:, j:j + 1], 0),
                                          tokno.bitcast(i32)[:, i:i + 1], None).then_inc(s_scat, 16)
            gp.wait_ge(s_scat, 16 * TT * TOPK)
            gp.wait_ge(s_hst, 16 * TT)
            gp.wait_ge(s_tab, 1)
            nb = gp.value_load(tab_i[0:1, N_BLOCKS:N_BLOCKS + 1], min_val=T * TOPK // P, max_val=N_BLOCKS)

            gp.memset(held[0:1, :], 0.0).then_inc(s_held, 1)

            def hold_waits(n):
                gp.wait_ge(s_held, n)
                gp.tensor_tensor(held[0:1, :], zeros[0:1, 0:1], zeros[0:1, 0:1], ALU.add).then_inc(s_held, 1)

            def gather(row, count, holds=None):
                gp.dma_start(idx_in.bitcast(i32), tokof[bass.ds(row, P), :]).then_inc(s_tk, 16)
                gp.wait_ge(s_tk, count)
                if holds is not None:
                    hold_waits(holds)
                gp.indirect_dma_start(xg, None, hrows, bass.IndirectOffsetOnAxis(idx_in.bitcast(mybir.dt.uint32), 0)).then_inc(s_ga, 16)

            gather(0, 16)
            with gp.Fori(0, nb) as b:
                gp.wait_ge(s_brow, b * 32 + 32)
                gp.wait_ge(s_y, b + 1)
                hold_waits(b * 2 + 1)
                gp.partition_broadcast(biasb, brow[0:1, :]).then_inc(s_bb, 1)
                gp.wait_ge(s_xtp, b * 2 + 2)
                gp.wait_ge(s_ga, b * 16 + 16)
                gather(b * P + P, b * 16 + 32, b * 2 + 2)
            gp.wait_ge(s_yst, nb * 16 + 32)
            for i in range(TT):
                for k in range(TOPK):
                    j = TOPK * i + k
                    if j == 0:
                        gp.wait_ge(s_used, nb * MT)
                        hold_waits(nb * 2 + 1)
                    if j >= 2:
                        gp.wait_ge(s_acc, j - 1)
                    gp.indirect_dma_start(yg[:, j % 2, :], None, yrows,
                                          bass.IndirectOffsetOnAxis(desti_u[:, j:j + 1], 0)).then_inc(s_yg[j % 2], 16)

        @block.tensor
        def _(pe):
            seen = set()

            def products(stage, first=None, last=None):
                a, b = stages[stage]
                for n in range(a, b):
                    groups, _ = pairs[n]
                    if n >= 2:
                        pe.wait_ge(s_evac, n - 1)
                    for m, (mm, rows, cols) in enumerate(groups):
                        bank = jb[2 * (n % 2) + m]
                        for i, (t, lhsT, rhs) in enumerate(mm):
                            if t not in seen:
                                seen.add(t)
                                pe.wait_ge(s_slot[t % RING], 16 * (t // RING + 1))
                            ins = nc.tensor.matmul(bank[0:rows, 0:cols], lhsT, rhs, start=(i == 0), stop=(i == len(mm) - 1))
                    ins.then_inc(s_pair, 1)

            def norm(name):
                n = NI[name]
                _, _, nch, w = NORMS[n]
                for c in range(nch):
                    g = chunk0[n] + c
                    pe.wait_ge(s_sq, g + 1)
                    nc.tensor.matmul(PT[:, 0:w], ones, sq[:, g % 2, 0:w], start=(c == 0), stop=(c == nch - 1)).then_inc(s_mm, 1)

            def rope(r):
                buf, _, _, rows = ROPES[r]
                if r >= 2:
                    pe.wait_ge(s_rope, r - 1)
                pe.wait_ge(s_rot_in, 1)
                nc.tensor.matmul(LB[r % 2][0:rows, :], rot[0:rows, 0:rows], buf, start=True, stop=True).then_inc(s_rot, 1)

            def scores(u):
                U = UNITS[u]
                if u:
                    pe.wait_ge(s_exp, u)
                for grp in U["sc"]:
                    for i, (l, r, a, b) in enumerate(grp):
                        ins = nc.tensor.matmul(S[:, a:b], l, r, start=(i == 0), stop=(i == len(grp) - 1))
                ins.then_inc(s_sc, 1)

            def values(u):
                U = UNITS[u]
                pe.wait_ge(s_prob, u + 1)
                nv = len(U["v"])
                pr = U["pr"][:, u % 2, :]
                for g in range((nv + 3) // 4):
                    t = turns0[u] + g
                    if t:
                        pe.wait_ge(s_trc, t)
                    for j in range(4 * g, min(4 * g + 4, nv)):
                        ins = nc.tensor.transpose(PT[:, P * (j % 4):P * (j % 4) + P], pr[:, P * j:P * j + P], ident)
                    ins.then_inc(s_tr, 1)
                if u:
                    pe.wait_ge(s_out, u)
                for g in range((nv + 3) // 4):
                    pe.wait_ge(s_trc, turns0[u] + g + 1)
                    for j in range(4 * g, min(4 * g + 4, nv)):
                        ins = nc.tensor.matmul(PO[:, 0:P], U["v"][j], U["pt"][:, P * j:P * j + P], start=(j == 0), stop=(j == nv - 1))
                ins.then_inc(s_pv, 1)

            def attention(a, b):
                scores(a)
                for u in range(a, b):
                    if u + 1 < b:
                        scores(u + 1)
                    values(u)

            pe.wait_ge(s_const, 32)
            norm("pre_mix")
            norm("mem")
            pe.wait_ge(s_norm, 1)
            products("in1")
            pe.wait_ge(s_norm, 2)
            products("mem")
            pe.wait_ge(s_evac, stages["in1"][1])
            for r in range(8):
                rope(r)
            pe.wait_ge(s_rope, 8)
            pe.wait_ge(s_evac, stages["mem"][1])
            attention(0, U_X)
            attention(U_X, U_M)
            norm("attn")
            norm("conv")
            norm("xattn")
            pe.wait_ge(s_norm, 5)
            products("out1")
            norm("post_mix")
            norm("pre_mlp")
            pe.wait_ge(s_norm, 6)
            products("up")
            pe.wait_ge(s_ffn, 16)
            products("down")
            norm("post_mlp")
            if stop == "x1":
                return
            pe.wait_ge(s_silu, 1)
            products("mod")
            norm("mix2")
            norm("ctx")
            pe.wait_ge(s_norm, 8)
            products("in2")
            norm("qin")
            norm("ckv_lat")
            norm("ckv_ctx")
            pe.wait_ge(s_evac, stages["in2"][1])
            rope(8)
            pe.wait_ge(s_norm, 11)
            for g in range(4):
                if g:
                    pe.wait_ge(s_out, U_M + 8 * g)
                products(f"mla{g}")
                pe.wait_ge(s_evac, stages[f"mla{g}"][1])
                for m in range(2):
                    rope(9 + 2 * g + m)
                pe.wait_ge(s_rope, 11 + 2 * g)
                attention(U_M + 8 * g, U_M + 8 * g + 8)
            n_kt = n_lev = 0
            for g in range(4):
                products(f"hg{g}")
                pe.wait_ge(s_evac, stages[f"hg{g}"][1])
                for m in range(2):
                    n = 2 * g + m
                    for d in range(2):
                        pe.wait_ge(s_kd, 2 * n + d + 1)
                        for c in range(AC):
                            ins = nc.tensor.transpose(S[:, P * c:P * c + P], E[:, d, P * c:P * c + P], ident)
                        ins.then_inc(s_kt, 1)
                        pe.wait_ge(s_ktc, 2 * n + d + 1)
                        for j in range(5):
                            c = SEQ[d][j]
                            dst = PT[:, P * j:P * j + P] if j < 4 else LB[1][:, 256:384]
                            ins = nc.tensor.matmul(dst, kT[:, c, :], hv[:, c, P * m:P * m + P], start=True, stop=True)
                        ins.then_inc(s_ds, 1)
                        pe.wait_ge(s_st, 2 * n + d + 1)
                    for L in range(15):
                        l = 15 * n + L
                        pe.wait_ge(s_x, l + 1)
                        if l >= 2:
                            pe.wait_ge(s_at, l - 1)
                        for c in range(TT):
                            cs_ = slice(P * c, P * c + P)
                            to = LB[L % 2][:, cs_]
                            if L < 14:
                                ins = nc.tensor.matmul(to, X[:, L % 2, cs_], X[:, L % 2, cs_], start=True, stop=True)
                            else:
                                nc.tensor.matmul(to, kk[:, 0, cs_], qq[:, cs_], start=True, stop=False)
                                ins = nc.tensor.matmul(to, kk[:, 1, cs_], qq[:, cs_], start=False, stop=True)
                        ins.then_inc(s_p, 1)
                    pe.wait_ge(s_at, 15 * n + 15)
                    for c in range(TT):
                        cs_ = slice(P * c, P * c + P)
                        nc.tensor.matmul(PO[:, cs_], St[:, 1 + c, :], qe[:, 0, cs_], start=True, stop=False)
                        nc.tensor.matmul(PO[:, cs_], St[:, 5 + 1 + (3 - c), :], qe[:, 1, cs_], start=False, stop=False)
                        ins = nc.tensor.matmul(PO[:, cs_], hv[:, c, P * m:P * m + P], At[:, cs_], start=False, stop=True)
                    ins.then_inc(s_o, 1)
                    norm(f"head{n}")
                    pe.wait_ge(s_hg, n + 1)
            products("out2")
            if dbg is not None:
                return
            norm("ffn2")
            pe.wait_ge(s_norm, 12)
            pe.wait_ge(s_route_w, 32)
            for i in range(TT):
                ts = slice(P * i, P * i + P)
                for c in range(DC):
                    nc.tensor.matmul(PO[:, N_EXP * i:N_EXP * i + N_EXP], h3[:, c, ts], wrs[:, c, :], start=(c == 0), stop=False)
                ins = nc.tensor.matmul(PO[:, N_EXP * i:N_EXP * i + N_EXP], ones[0:1, :], brs[0:1, :], start=False, stop=True)
            ins.then_inc(s_lgp, 1)
            for i in range(TT):
                if i:
                    pe.wait_ge(s_hc, i)
                for c in range(DC):
                    ins = nc.tensor.transpose(S[:, P * c:P * c + P], h3[:, c, P * i:P * i + P], ident)
                ins.then_inc(s_hT, 1)
            pe.wait_ge(s_mem, 1)
            for i in range(TT):
                to = PO[:, 128 + N_EXP * i:128 + N_EXP * i + N_EXP]
                for j in range(i):
                    nc.tensor.matmul(to, ones, member[:, j, :], start=(j == 0), stop=False)
                nc.tensor.matmul(to, const("tri"), member[:, i, :], start=(i == 0), stop=True)
            for j in range(TT):
                ins = nc.tensor.matmul(PO[:, 256:256 + N_EXP], ones, member[:, j, :], start=(j == 0), stop=(j == TT - 1))
            ins.then_inc(s_rank, 1)
            pe.wait_ge(s_tab, 1)
            nb = pe.value_load(tab_i[0:1, N_BLOCKS:N_BLOCKS + 1], min_val=T * TOPK // P, max_val=N_BLOCKS)

            def turn(src, dst, signal):
                for c in range(4):
                    ins = nc.tensor.transpose(dst[:, P * c:P * c + P], src[:, P * c:P * c + P], ident)
                ins.then_inc(signal, 1)

            pe.wait_ge(s_ga, 16)
            turn(xg[:, 0:512], PT, s_xtp)
            pe.wait_ge(s_xtc, 1)
            turn(xg[:, 512:1024], PT, s_xtp)
            with pe.Fori(0, nb) as b:
                pe.wait_ge(s_xtc, b * 2 + 2)
                for hf in range(2):
                    for k in range(DC):
                        t = 8 * hf + k
                        pe.wait_ge(s_w[t], b * 16 + 16)
                        for j in range(2):
                            ins = nc.tensor.matmul(jb[2 * hf + j], xTb[:, k, :], mw[:, t, 512 * j:512 * j + 512],
                                                   start=(k == 0), stop=(k == DC - 1))
                        ins.then_inc(s_used, 1)
                pe.wait_ge(s_actr, b * 2 + 1)
                turn(actb[:, 0:512], PT, s_atp)
                pe.wait_ge(s_y, b + 1)
                for k in range(DC):
                    if k == 0:
                        pe.wait_ge(s_atc, b * 2 + 1)
                    if k == 4:
                        pe.wait_ge(s_actr, b * 2 + 2)
                        turn(actb[:, 512:1024], PO, s_atp)
                        pe.wait_ge(s_ga, b * 16 + 32)
                        turn(xg[:, 0:512], PT, s_xtp)
                        pe.wait_ge(s_atc, b * 2 + 2)
                    if k == 6:
                        pe.wait_ge(s_xtc, b * 2 + 3)
                        turn(xg[:, 512:1024], PT, s_xtp)
                    pe.wait_ge(s_w[16 + k], b * 16 + 16)
                    for j in range(2):
                        ins = nc.tensor.matmul(S[:, 512 * j:512 * j + 512], aT[:, k, :], mw[:, 16 + k, 512 * j:512 * j + 512],
                                               start=(k == 0), stop=(k == DC - 1))
                    ins.then_inc(s_used, 1)
            pe.wait_ge(s_y, nb + 1)
            for i in range(TT):
                pe.wait_ge(s_acc, TOPK * i + TOPK)
                if i:
                    pe.wait_ge(s_tTc, i)
                for c in range(DC):
                    ins = nc.tensor.transpose(S[:, P * c:P * c + P], acc[:, i, P * c:P * c + P], ident)
                ins.then_inc(s_tT, 1)
            norm("final")

        @block.scalar
        def _(act):
            steps = [0]

            def link(ins):
                steps[0] += 1
                ins.then_inc(s_act, 1)
                act.wait_ge(s_act, steps[0])

            def evacuate(stage):
                a, b = stages[stage]
                for n in range(a, b):
                    act.wait_ge(s_pair, n + 1)
                    for m, (dst, func, scale, bias, rows, cols) in enumerate(pairs[n][1]):
                        src = jb[2 * (n % 2) + m][0:rows, 0:cols]
                        ins = nc.scalar.activation(dst, src, func, bias=bias, scale=scale)
                    ins.then_inc(s_evac, 1)

            def norm_root(name):
                n = NI[name]
                w = NORMS[n][3]
                act.wait_ge(s_ms, n + 1)
                nc.scalar.activation(ms[:, 0:w], ms[:, 0:w], F.Sqrt).then_inc(s_rt, 1)

            def exps(u):
                U = UNITS[u]
                act.wait_ge(s_max, u + 1)
                src = masked[:, 0:U["nk"]] if U["mask"] is not None else S[:, 0:U["nk"]]
                scale = 1.0 if U["mask"] is not None else U["scale"]
                nc.scalar.activation(U["pr"][:, u % 2, 0:U["nk"]], src, F.Exp, bias=small[:, u % 2:u % 2 + 1], scale=scale,
                                     accum_out=small[:, 2 + u % 2:3 + u % 2]).then_inc(s_exp, 1)

            def attention(a, b):
                exps(a)
                for u in range(a, b):
                    U = UNITS[u]
                    nv = len(U["v"])
                    for g in range((nv + 3) // 4):
                        w = P * min(4, nv - 4 * g)
                        act.wait_ge(s_tr, turns0[u] + g + 1)
                        nc.scalar.activation(U["pt"][:, 512 * g:512 * g + w], PT[:, 0:w], F.Copy).then_inc(s_trc, 1)
                    if u + 1 < b:
                        exps(u + 1)
                    act.wait_ge(s_pv, u + 1)
                    nc.scalar.activation(U["dst"], PO[U["rows"], 0:P], F.Copy).then_inc(s_out, 1)

            act.wait_ge(s_zero, 1)
            for half in range(2):
                act.dma_start(yrows[:, 512 * half:512 * half + 512].rearrange("(p b) n -> p b n", p=P),
                              zeros.unsqueeze(1).broadcast_to([P, N_ROWS // P, 512])).then_inc(s_yst, 16)
            norm_root("pre_mix")
            norm_root("mem")
            act.wait_ge(s_ang, 1)
            nc.scalar.activation(sinT, trn, F.Sin).then_inc(s_sin, 1)
            act.wait_ge(s_ang, 2)
            nc.scalar.activation(cosT, ang, F.Sin).then_inc(s_sin, 1)
            evacuate("in1")
            evacuate("mem")
            attention(0, U_X)
            attention(U_X, U_M)
            for n in ("attn", "conv", "xattn"):
                norm_root(n)
            evacuate("out1")
            norm_root("post_mix")
            norm_root("pre_mlp")
            evacuate("up")
            evacuate("down")
            norm_root("post_mlp")
            if stop == "x1":
                return
            act.wait_ge(s_silc, 1)
            nc.scalar.activation(small[:, 16:32], vcol("c_2", 0, 16), F.Sigmoid).then_inc(s_silc, 1)
            evacuate("mod")
            norm_root("mix2")
            norm_root("ctx")
            evacuate("in2")
            for n in ("qin", "ckv_lat", "ckv_ctx"):
                norm_root(n)
            for g in range(4):
                evacuate(f"mla{g}")
                attention(U_M + 8 * g, U_M + 8 * g + 8)
            act.wait_ge(s_lb, 1)
            nc.scalar.activation(small[:, 96:128], small[:, 96:128], F.Exp).then_inc(s_lbe, 1)
            for g in range(4):
                evacuate(f"hg{g}")
                for m in range(2):
                    n = 2 * g + m
                    link(nc.scalar.activation(E[:, 0, 0:T], hq[:, m, :], F.Sigmoid))
                    nc.scalar.activation(E[:, 1, 0:T], hg[:, m, :], F.Sigmoid).then_inc(s_sil, 1)
                    for d in range(2):
                        act.wait_ge(s_f, 2 * n + d + 1)
                        link(nc.scalar.activation(lnA, lnA, F.Ln))
                        z = zs[:, 2 * d + m, :]
                        nc.scalar.activation(z, z, F.Ln).then_inc(s_ln, 1)
                        act.wait_ge(s_cum, 2 * n + d + 1)
                        link(nc.scalar.activation(E[:, d, :], dlt[:, d, :], F.Exp, scale=-1.0))
                        link(nc.scalar.activation(X[:, d, :], cum[:, d, 0:T], F.Exp))
                        ends = v3(cum[:, d, :], AC)[:, :, P - 1 if d == 0 else 0]
                        nc.scalar.activation(el[:, d, :], ends, F.Exp).then_inc(s_ec, 1)
                        act.wait_ge(s_kt, 2 * n + d + 1)
                        nc.scalar.activation(kT.rearrange("p a b -> p (a b)"), S[:, 0:TA], F.Copy).then_inc(s_ktc, 1)
                    for L in range(14):
                        l = 14 * n + L
                        act.wait_ge(s_d, l + 1)
                        hf = level_half[L % LEVELS]
                        fwd = L < LEVELS
                        dv = dlt[:, L % 2, 0:T].rearrange("p (b s) -> p b s", s=2 * hf)
                        ev = E[:, L % 2, 0:T].rearrange("p (b s) -> p b s", s=2 * hf)
                        up, lo = slice(hf, 2 * hf), slice(0, hf)
                        qh, kh = (up, lo) if fwd else (lo, up)
                        link(nc.scalar.activation(ev[:, :, qh], dv[:, :, qh], F.Exp))
                        nc.scalar.activation(ev[:, :, kh], dv[:, :, kh], F.Exp, scale=-1.0).then_inc(s_e, 1)
                    act.wait_ge(s_o, n + 1)
                    nc.scalar.activation(osb, PO[:, :], F.Copy).then_inc(s_osb, 1)
                    norm_root(f"head{n}")
            evacuate("out2")
            if dbg is not None:
                return
            norm_root("ffn2")
            act.wait_ge(s_top, 1)
            for i in range(TT):
                ins = nc.scalar.activation(prob[:, 4 * i:4 * i + 4], top8[:, i, 0:4], F.Exp, bias=small[:, 144 + i:145 + i],
                                           accum_out=small[:, 148 + i:149 + i])
            ins.then_inc(s_tope, 1)
            for i in range(TT):
                act.wait_ge(s_hT, i + 1)
                nc.scalar.activation(hr[:, i, :], S[:, :], F.Copy).then_inc(s_hc, 1)
            act.wait_ge(s_tab, 1)
            nb = act.value_load(tab_i[0:1, N_BLOCKS:N_BLOCKS + 1], min_val=T * TOPK // P, max_val=N_BLOCKS)

            def copy_turned(n, src, at, signal_in, signal, dst):
                act.wait_ge(signal_in, n)
                d = dst.rearrange("p a b -> p (a b)")[:, 512 * at:512 * at + 512]
                nc.scalar.activation(d, src[:, :], F.Copy).then_inc(signal, 1)

            copy_turned(1, PT, 0, s_xtp, s_xtc, xTb)
            copy_turned(2, PT, 1, s_xtp, s_xtc, xTb)
            with act.Fori(0, nb) as b:
                act.wait_ge(s_glu, b * 2 + 1)
                nc.scalar.activation(sig, glu, F.Sigmoid, scale=1.702).then_inc(s_sig, 1)
                copy_turned(b * 2 + 1, PT, 0, s_atp, s_atc, aT)
                act.wait_ge(s_glu, b * 2 + 2)
                nc.scalar.activation(sig, glu, F.Sigmoid, scale=1.702).then_inc(s_sig, 1)
                copy_turned(b * 2 + 2, PO, 1, s_atp, s_atc, aT)
                copy_turned(b * 2 + 3, PT, 0, s_xtp, s_xtc, xTb)
                copy_turned(b * 2 + 4, PT, 1, s_xtp, s_xtc, xTb)
                act.wait_ge(s_y, b + 2)
                act.dma_start(yrows[bass.ds(b * P, P), :], yb).then_inc(s_yst, 16)
            for i in range(TT):
                act.wait_ge(s_tT, i + 1)
                nc.scalar.activation(yT[:, :, P * i:P * i + P], v3(S[:, :], DC), F.Copy).then_inc(s_tTc, 1)
            norm_root("final")

        @block.vector
        def _(dve):
            steps = [0]
            V = nc.vector

            def link(ins):
                steps[0] += 1
                ins.then_inc(s_vec, 1)
                dve.wait_ge(s_vec, steps[0])

            def norm_stats(name, dim=None):
                n = NI[name]
                _, src, nch, w = NORMS[n]
                for c in range(nch):
                    g = chunk0[n] + c
                    if g >= 2:
                        dve.wait_ge(s_mm, g - 1)
                    V.tensor_tensor(sq[:, g % 2, 0:w], src[:, c, 0:w], src[:, c, 0:w], ALU.mult).then_inc(s_sq, 1)
                dve.wait_ge(s_mm, chunk0[n] + nch)
                V.tensor_scalar(ms[:, 0:w], PT[:, 0:w], 1.0 / (P * nch), EPS, ALU.mult, ALU.add).then_inc(s_ms, 1)
                dve.wait_ge(s_rt, n + 1)
                link(V.reciprocal(rstd[:, 0:w], ms[:, 0:w]))

            def norm_apply(name, dst, gain):
                _, src, nch, w = NORMS[NI[name]]
                for c in range(nch):
                    ins = V.scalar_tensor_tensor(dst[:, c, 0:w], src[:, c, 0:w], gain(c), rstd[:, 0:w], ALU.mult, ALU.mult)
                ins.then_inc(s_norm, 1)

            def norm(name, dst, vname):
                norm_stats(name)
                norm_apply(name, dst, lambda c: vcol(vname, c))

            def rope(r):
                buf, co, si, rows = ROPES[r]
                dve.wait_ge(s_rot, r + 1)
                if r:
                    dve.wait_ge(s_rope, r)
                t = tmp2 if r >= 8 else ang
                link(V.tensor_tensor(t[0:rows, :], LB[r % 2][0:rows, :], si, ALU.mult))
                link(V.tensor_tensor(buf, buf, co, ALU.mult))
                V.tensor_tensor(buf, buf, t[0:rows, :], ALU.add).then_inc(s_rope, 1)

            def maxes(u):
                U = UNITS[u]
                dve.wait_ge(s_sc, u + 1)
                nk = U["nk"]
                nm = small[:, u % 2:u % 2 + 1]
                if U["mask"] is not None:
                    link(V.scalar_tensor_tensor(masked[:, 0:nk], S[:, 0:nk], U["scale"], U["mask"], ALU.mult, ALU.add))
                    link(V.tensor_reduce(nm, masked[:, 0:nk], AX.X, ALU.max))
                    V.tensor_scalar(nm, nm, -1.0, None, ALU.mult).then_inc(s_max, 1)
                else:
                    link(V.tensor_reduce(nm, S[:, 0:nk], AX.X, ALU.max))
                    V.tensor_scalar(nm, nm, -U["scale"], None, ALU.mult).then_inc(s_max, 1)

            def attention(a, b):
                maxes(a)
                for u in range(a, b):
                    U = UNITS[u]
                    dve.wait_ge(s_exp, u + 1)
                    link(V.reciprocal(small[:, 4:5], small[:, 2 + u % 2:3 + u % 2]))
                    pr = U["pr"][:, u % 2, 0:U["nk"]]
                    V.tensor_scalar(pr, pr, small[:, 4:5], None, ALU.mult).then_inc(s_prob, 1)
                    if u + 1 < b:
                        maxes(u + 1)

            dve.wait_ge(s_const, 32)
            dve.wait_ge(s_in, 16)
            norm("pre_mix", h, "g_pre_mix")
            dve.wait_ge(s_tok, 16)
            norm("mem", hm, "g_mem")
            dve.wait_ge(s_pos, 16)
            link(V.tensor_copy(cosT, ang.bitcast(i32)))
            link(V.tensor_scalar(cosT, cosT, const("inv_freq"), None, ALU.mult))
            magic = 12582912.0
            link(V.tensor_scalar(sinT, cosT, 1.0 / (2 * np.pi), magic, ALU.mult, ALU.add))
            link(V.tensor_scalar(sinT, sinT, -magic, None, ALU.add))
            link(V.scalar_tensor_tensor(trn, sinT, -6.28125, cosT, ALU.mult, ALU.add))
            link(V.scalar_tensor_tensor(trn, sinT, -0.0019350051879882812, trn, ALU.mult, ALU.add))
            link(V.scalar_tensor_tensor(trn, sinT, -3.019916050561733e-07, trn, ALU.mult, ALU.add))
            PI = 3.1415925
            link(V.tensor_scalar(ang, trn, float(np.pi / 2), -2 * float(np.pi), ALU.is_gt, ALU.mult))
            link(V.scalar_tensor_tensor(ang, trn, float(np.pi / 2), ang, ALU.add, ALU.add))
            link(V.tensor_scalar(ang, ang, PI, -PI, ALU.min, ALU.max))
            V.tensor_scalar(trn, trn, PI, -PI, ALU.min, ALU.max).then_inc(s_ang, 2)
            dve.wait_ge(s_sin, 2)
            dve.wait_ge(s_evac, stages["in1"][1])
            V.memset(small[:, 8:9], 0.0).then_inc(s_rot_in, 1)
            for r in range(8):
                rope(r)
            attention(0, U_X)
            for c in range(2):
                w = lambda tap: vcol("conv_w", 2 * tap + c)
                link(V.tensor_tensor(cc[:, c, :], cc[:, c, :], cu[:, c, :], ALU.mult))
                z, y = cc[:, c, :], yconv[:, c, :]
                link(V.tensor_scalar(y, z, w(2), None, ALU.mult))
                link(V.scalar_tensor_tensor(y[:, 1:T], z[:, 0:T - 1], w(1), y[:, 1:T], ALU.mult, ALU.add))
                link(V.scalar_tensor_tensor(y[:, 2:T], z[:, 0:T - 2], w(0), y[:, 2:T], ALU.mult, ALU.add))
                link(V.tensor_tensor(y, y, cb[:, c, :], ALU.mult))
            attention(U_X, U_M)
            dve.wait_ge(s_out, U_M)
            norm("attn", h[:, 0:4, :], "g_attn_out")
            norm("conv", h[:, 4:6, :], "g_conv_out")
            norm("xattn", h[:, 6:8, :], "g_xattn_out")
            dve.wait_ge(s_evac, stages["out1"][1])

            def add_normed(name, gain):
                norm_stats(name)
                _, src, nch, w = NORMS[NI[name]]
                for c in range(nch):
                    link(V.scalar_tensor_tensor(src[:, c, :], src[:, c, :], gain(c), rstd[:, :], ALU.mult, ALU.mult))
                    link(V.tensor_tensor(x[:, c, :], x[:, c, :], src[:, c, :], ALU.add))

            add_normed("post_mix", lambda c: vcol("g_post_mix", c))
            norm("pre_mlp", h, "g_pre_mlp")
            for i in range(16):
                dve.wait_ge(s_evac, stages["up"][0] + i + 1)
                f = ffn[:, 2 * i:2 * i + 2, :]
                V.tensor_tensor(f, f, f, ALU.mult).then_inc(s_ffn, 1)
            dve.wait_ge(s_evac, stages["down"][1])
            add_normed("post_mlp", lambda c: vcol("g_post_mlp", c))
            V.memset(small[:, 8:9], 0.0).then_inc(s_res, 1)
            if stop == "x1":
                return
            V.memset(small[:, 9:10], 0.0).then_inc(s_silc, 1)
            dve.wait_ge(s_silc, 2)
            for j, nm in enumerate(("c_2", "c_ctx_2")):
                ins = V.tensor_tensor(v3(cs, 8)[:, :, j], small[:, 16 + 8 * j:24 + 8 * j], vcol(nm, 0, 8), ALU.mult)
            ins.then_inc(s_silu, 1)
            dve.wait_ge(s_evac, stages["mod"][1])
            gm = small[:, 32:56].rearrange("p (a b) -> p a b", a=3)
            for j, (part, who, nm) in enumerate(((1, 0, "norm_mix_g_2"), (1, 1, "norm_mix_g_2"), (4, 0, "norm_ffn_g_2"))):
                link(V.scalar_tensor_tensor(gm[:, j, :], modv[:, 8 * part:8 * part + 8, who], 1.0, vcol(nm, 0, 8), ALU.add, ALU.mult))

            def modulated(name, dst, j, shift, who):
                norm_stats(name)
                _, src, nch, w = NORMS[NI[name]]
                for c in range(nch):
                    link(V.scalar_tensor_tensor(dst[:, c, 0:w], src[:, c, 0:w], gm[:, j, c:c + 1], rstd[:, 0:w], ALU.mult, ALU.mult))
                    ins = V.tensor_scalar(dst[:, c, 0:w], dst[:, c, 0:w], modv[:, 8 * shift + c, who:who + 1], None, ALU.add)
                    if c < nch - 1:
                        link(ins)
                ins.then_inc(s_norm, 1)

            modulated("mix2", ha, 0, 0, 0)
            dve.wait_ge(s_tok, 32)
            modulated("ctx", hctx, 1, 0, 1)
            dve.wait_ge(s_evac, stages["in2"][1])
            norm("qin", qin, "mla_q_norm_g_2")
            norm("ckv_lat", ckv, "mla_kv_norm_g_2")
            norm("ckv_ctx", ckv[:, :, T:TA], "mla_kv_norm_g_2")
            rope(8)
            for g in range(4):
                dve.wait_ge(s_evac, stages[f"mla{g}"][1])
                for m in range(2):
                    rope(9 + 2 * g + m)
                attention(U_M + 8 * g, U_M + 8 * g + 8)
            lbv = vcol("hg_lb_logits_2", 0, 32).rearrange("p (d l c) -> p d l c", d=2, l=2)
            lbe = small[:, 96:128].rearrange("p (d l c) -> p d l c", d=2, l=2)
            lb = small[:, 128:144].rearrange("p (d c) -> p d c", d=2)
            olb = small[:, 56:72].rearrange("p (d c) -> p d c", d=2)
            link(V.tensor_tensor(lb, lbv[:, :, 0, :], lbv[:, :, 1, :], ALU.max))
            link(V.tensor_tensor(lbe[:, :, 0, :], lbv[:, :, 0, :], lb, ALU.subtract))
            V.tensor_tensor(lbe[:, :, 1, :], lbv[:, :, 1, :], lb, ALU.subtract).then_inc(s_lb, 1)
            dve.wait_ge(s_lbe, 1)
            link(V.tensor_tensor(olb, lbe[:, :, 0, :], lbe[:, :, 1, :], ALU.add))
            link(V.reciprocal(olb, olb))
            link(V.tensor_tensor(lb, lbe[:, :, 0, :], olb, ALU.mult))
            link(V.tensor_scalar(olb, lb, -1.0, 1.0, ALU.mult, ALU.add))
            for g in range(4):
                dve.wait_ge(s_evac, stages[f"hg{g}"][1])
                for m in range(2):
                    n = 2 * g + m
                    dve.wait_ge(s_sil, n + 1)
                    link(V.scalar_tensor_tensor(qq, hq[:, m, :], P ** -0.5, E[:, 0, 0:T], ALU.mult, ALU.mult))
                    link(V.tensor_tensor(hg[:, m, :], hg[:, m, :], E[:, 1, 0:T], ALU.mult))
                    for d in range(2):
                        z = zs[:, 2 * d + m, :]
                        link(V.tensor_scalar(z, z, olb[:, d, n:n + 1], lb[:, d, n:n + 1], ALU.mult, ALU.add))
                        link(V.tensor_scalar(kk[:, d, :], z, -1.0, 1.0, ALU.mult, ALU.add))
                        link(V.tensor_scalar(lnA, z, 2.0 ** -63, None, ALU.max))
                        V.tensor_scalar(z, z, 2.0 ** 63, 1.0, ALU.mult, ALU.min).then_inc(s_f, 1)
                        dve.wait_ge(s_ln, 2 * n + d + 1)
                        link(V.tensor_tensor(z, z, lnA, ALU.add))
                        cd = cum[:, d, :]
                        if d == 0:
                            link(V.tensor_tensor_scan(cd, const("reset"), z, 0.0, ALU.mult, ALU.add))
                        else:
                            link(V.tensor_tensor_scan(cd[:, ::-1], const("reset"), z[:, ::-1], 0.0, ALU.mult, ALU.add))
                        c3 = v3(cd, AC)
                        far = c3[:, :, P - 1:P] if d == 0 else c3[:, :, 0:1]
                        V.tensor_tensor(v3(dlt[:, d, :], AC), c3, far.broadcast_to([P, AC, P]), ALU.subtract).then_inc(s_cum, 1)
                        dve.wait_ge(s_ec, 2 * n + d + 1)
                        link(V.tensor_tensor(qe[:, d, :], qq, X[:, d, :], ALU.mult))
                        V.tensor_tensor(E[:, d, :], E[:, d, :], kk[:, d, :], ALU.mult).then_inc(s_kd, 1)
                        dve.wait_ge(s_ds, 2 * n + d + 1)
                        link(V.tensor_copy(St[:, 5 * d, :], PT[:, 0:P]))
                        for j in range(1, 5):
                            src = PT[:, P * j:P * j + P] if j < 4 else LB[1][:, 256:384]
                            c = SEQ[d][j]
                            ins = V.scalar_tensor_tensor(St[:, 5 * d + j, :], St[:, 5 * d + j - 1, :], el[:, d, c:c + 1], src,
                                                         ALU.mult, ALU.add)
                            if j < 4:
                                link(ins)
                        ins.then_inc(s_st, 1)

                    def views(a, hf):
                        return a.rearrange("p (b s) -> p b s", s=2 * hf)

                    def difference(L):
                        hf, d = level_half[L % LEVELS], L // LEVELS
                        c3 = views(cum[:, d, 0:T], hf)
                        ref = c3[:, :, hf - 1:hf] if d == 0 else c3[:, :, hf:hf + 1]
                        nb = T // (2 * hf)
                        V.tensor_tensor(views(dlt[:, L % 2, 0:T], hf), c3, ref.broadcast_to([P, nb, 2 * hf]),
                                        ALU.subtract).then_inc(s_d, 1)

                    def gather(L):
                        dve.wait_ge(s_p, 15 * n + L + 1)
                        if 15 * n + L:
                            dve.wait_ge(s_at, 15 * n + L)
                        mk = level_masks[:, L:L + 1, :].broadcast_to([P, TT, P])
                        V.copy_predicated(v3(At, TT), mk, v3(LB[L % 2], TT)).then_inc(s_at, 1)

                    difference(0)
                    for L in range(14):
                        if L < 13:
                            if L >= 1:
                                pass
                            difference(L + 1)
                        dve.wait_ge(s_e, 14 * n + L + 1)
                        hf, d = level_half[L % LEVELS], L // LEVELS
                        up, lo = slice(hf, 2 * hf), slice(0, hf)
                        qh, kh = (up, lo) if d == 0 else (lo, up)
                        ev, xv = views(E[:, L % 2, 0:T], hf), views(X[:, L % 2, :], hf)
                        link(V.tensor_tensor(xv[:, :, qh], ev[:, :, qh], views(qq, hf)[:, :, qh], ALU.mult))
                        V.tensor_tensor(xv[:, :, kh], ev[:, :, kh], views(kk[:, d, 0:T], hf)[:, :, kh], ALU.mult).then_inc(s_x, 1)
                        if L >= 1:
                            gather(L - 1)
                    V.memset(small[:, 8:9], 0.0).then_inc(s_x, 1)
                    gather(13)
                    gather(14)
                    dve.wait_ge(s_osb, n + 1)
                    norm_stats(f"head{n}")
                    link(V.scalar_tensor_tensor(osb, osb, vcol("hg_norm_g_2"), rstd[:, :], ALU.mult, ALU.mult))
                    link(V.tensor_tensor(osb, osb, hg[:, m, :], ALU.mult))
                    link(V.tensor_tensor(osb, osb, s8[:, m, :], ALU.mult))
                    link(V.tensor_tensor(ymla[:, n, :], ymla[:, n, :], s7[:, m, :], ALU.mult))
                    V.tensor_tensor(ymla[:, n, :], ymla[:, n, :], osb, ALU.add).then_inc(s_hg, 1)
            dve.wait_ge(s_evac, stages["out2"][1])
            for c in range(DC):
                ins = V.scalar_tensor_tensor(x[:, c, :], mout2[:, c, :], modv[:, 16 + c, 0:1], x[:, c, :], ALU.mult, ALU.add)
                if c < DC - 1:
                    link(ins)
            ins.then_inc(s_res, 1)
            if dbg is not None:
                return
            dve.wait_ge(s_res, 2)
            modulated("ffn2", h3, 2, 3, 0)
            dve.wait_ge(s_lgp, 1)
            link(V.tensor_copy(lg, v3(PO[:, 0:TT * N_EXP], TT)))
            for i in range(TT):
                link(V.max(top8[:, i, :], lg[:, i, :]))
                link(V.max_index(idx8.bitcast(mybir.dt.uint32)[:, i, :], top8[:, i, :], lg[:, i, :]))
            V.tensor_scalar(small[:, 144:148], top8[:, :, 0], -1.0, None, ALU.mult).then_inc(s_top, 1)
            link(V.tensor_copy(idxf, idx8.bitcast(mybir.dt.uint32)[:, :, 0:4]))
            hot3 = hot.rearrange("p (a e) -> p a e", e=N_EXP)
            en = const("expert_no").unsqueeze(1).broadcast_to([P, 16, N_EXP])
            i3 = idxf.rearrange("p a b -> p (a b)").unsqueeze(2).broadcast_to([P, 16, N_EXP])
            link(V.tensor_tensor(hot3, en, i3, ALU.is_equal))
            V.tensor_reduce(member, hot.rearrange("p (i k e) -> p i e k", i=TT, k=TOPK), AX.X, ALU.add).then_inc(s_mem, 1)
            dve.wait_ge(s_tope, 1)
            link(V.reciprocal(small[:, 152:156], small[:, 148:152]))
            for i in range(TT):
                link(V.tensor_scalar(prob[:, 4 * i:4 * i + 4], prob[:, 4 * i:4 * i + 4], small[:, 152 + i:153 + i], None, ALU.mult))
            dve.wait_ge(s_rank, 1)
            link(V.tensor_scalar(blocks_of, PO[:, 256:256 + N_EXP], 1.0 / P, (P - 1) / (2.0 * P), ALU.mult, ALU.add))
            link(V.tensor_scalar(blocks_of, blocks_of, magic, -magic, ALU.add, ALU.add))
            link(V.tensor_tensor_scan(block_end, ones[:, 0:N_EXP], blocks_of, 0.0, ALU.mult, ALU.add))
            link(V.tensor_tensor(first_row, block_end, blocks_of, ALU.subtract))
            link(V.tensor_scalar(first_row, first_row, float(P), None, ALU.mult))
            link(V.tensor_tensor(rank, v3(PO[:, 128:128 + TT * N_EXP], TT), first_row.unsqueeze(1).broadcast_to([P, TT, N_EXP]), ALU.add))
            for i in range(TT):
                a = hot2.rearrange("p (i k e) -> p i k e", i=TT, k=TOPK)[:, i]
                h_ = hot.rearrange("p (i k e) -> p i k e", i=TT, k=TOPK)[:, i]
                link(V.tensor_tensor(a, h_, rank[:, i:i + 1, :].broadcast_to([P, TOPK, N_EXP]), ALU.mult))
            link(V.tensor_reduce(destf, hot2.rearrange("p (a e) -> p a e", e=N_EXP), AX.X, ALU.add))
            link(V.tensor_copy(tokno.bitcast(i32), const("token_no")))
            V.tensor_copy(desti.bitcast(i32), destf).then_inc(s_dest, 1)
            cm = cmpb[0:1, :].rearrange("p (b e) -> p b e", e=N_EXP)
            link(V.tensor_tensor(cm, block_end[0:1, :].unsqueeze(1).broadcast_to([1, N_BLOCKS, N_EXP]),
                                 const("block_no")[0:1, :].unsqueeze(2).broadcast_to([1, N_BLOCKS, N_EXP]), ALU.is_le))
            link(V.tensor_reduce(block_expert[0:1, :], cm, AX.X, ALU.add))
            link(V.tensor_scalar(tab_i[0:1, 0:N_BLOCKS], block_expert[0:1, :], float(N_EXP - 1), None, ALU.min))
            V.tensor_copy(tab_i[0:1, N_BLOCKS:N_BLOCKS + 1], block_end[0:1, N_EXP - 1:N_EXP]).then_inc(s_tab, 1)
            dve.wait_ge(s_tab, 1)
            nb = dve.value_load(tab_i[0:1, N_BLOCKS:N_BLOCKS + 1], min_val=T * TOPK // P, max_val=N_BLOCKS)
            LOOP_STEPS = 5
            V.memset(small[:, 9:10], 0.0).then_inc(s_y, 1)
            with dve.Fori(0, nb) as b:
                done = [0]

                def step(ins):
                    done[0] += 1
                    ins.then_inc(s_vl, 1)
                    dve.wait_ge(s_vl, b * LOOP_STEPS + done[0])

                dve.wait_ge(s_bb, b + 1)
                for hf in range(2):
                    dve.wait_ge(s_used, b * MT + 8 * (hf + 1))
                    step(V.tensor_tensor(tbuf, G[:, 1024 * hf:1024 * hf + 1024], biasb[:, 1024 * hf:1024 * hf + 1024], ALU.add))
                    pr = tbuf.rearrange("p (n two) -> p n two", two=2)
                    V.tensor_scalar(glu, pr[:, :, 0], 7.0, None, ALU.min).then_inc(s_glu, 1)
                    step(V.tensor_scalar(lin, pr[:, :, 1], 7.0, -7.0, ALU.min, ALU.max))
                    dve.wait_ge(s_glu, b * 2 + hf + 1)
                    a = actb[:, 512 * hf:512 * hf + 512]
                    V.scalar_tensor_tensor(lin, lin, 1.0, glu, ALU.add, ALU.mult).then_inc(s_lg, 1)
                    dve.wait_ge(s_lg, b * 2 + hf + 1)
                    dve.wait_ge(s_sig, b * 2 + hf + 1)
                    V.tensor_tensor(a, lin, sig, ALU.mult).then_inc(s_actr, 1)
                    dve.wait_ge(s_actr, b * 2 + hf + 1)
                dve.wait_ge(s_used, b * MT + MT)
                dve.wait_ge(s_yst, b * 16 + 32)
                step(V.tensor_tensor(yb, S[:, :], biasb[:, 2048:3072], ALU.add))
                V.memset(small[:, 9:10], 0.0).then_inc(s_y, 1)
                dve.wait_ge(s_y, b + 2)
            for i in range(TT):
                for k in range(TOPK):
                    j = TOPK * i + k
                    dve.wait_ge(s_yg[j % 2], 16 * (j // 2 + 1))
                    w = prob[:, j:j + 1]
                    if k == 0:
                        V.tensor_scalar(acc[:, i, :], yg[:, j % 2, :], w, None, ALU.mult).then_inc(s_acc, 1)
                    else:
                        dve.wait_ge(s_acc, j)
                        V.scalar_tensor_tensor(acc[:, i, :], yg[:, j % 2, :], w, acc[:, i, :], ALU.mult, ALU.add).then_inc(s_acc, 1)
            dve.wait_ge(s_tTc, TT)
            for c in range(DC):
                link(V.scalar_tensor_tensor(x[:, c, :], yT[:, c, :], modv[:, 40 + c, 0:1], x[:, c, :], ALU.mult, ALU.add))
            norm("final", fin, "final_norm_g_2")


def constants():
    c = np.zeros((P, N_CONST), np.float32)

    def put(name, a):
        c[:, CONST_AT[name]:CONST_AT[name] + dict(CONSTS)[name]] = a

    put("ident", np.eye(P, dtype=np.float32))
    put("ones", 1.0)
    r = np.zeros((P, P), np.float32)
    for b in (0, 64):
        for i in range(32):
            r[b + i + 32, b + i] = -1.0
            r[b + i, b + i + 32] = 1.0
    put("rot", r)
    d = np.arange(P)[:, None] + (T - P) - np.arange(T)[None, :]
    n = ((d >= 0) & (d <= 128)).astype(int) + ((d >= 0) & (d % 4 == 0)) + ((d >= 0) & (d % 16 == 0))
    put("band", np.where(n > 0, np.log(np.maximum(n, 1)), NEG))
    lv = np.zeros((P, 15, P), np.uint8)
    s, t = np.arange(P)[:, None], np.arange(P)[None, :]
    for i in range(LEVELS):
        hf = P >> (i + 1)
        same = (s // (2 * hf)) == (t // (2 * hf))
        lv[:, i] = same & (s % (2 * hf) < hf) & (t % (2 * hf) >= hf)
        lv[:, LEVELS + i] = lv[:, i].T
    lv[:, 14] = s == t
    put("levels", lv.reshape(P, -1).view(np.float32))
    put("reset", (np.arange(TA) % P != 0).astype(np.float32))
    half = DH1 // 2
    inv = np.float32(10000.0) ** (-(np.arange(half, dtype=np.float32) * np.float32(2.0) / np.float32(DH1)))
    put("inv_freq", np.tile(inv.astype(np.float32), 4)[:, None])
    row, col = np.repeat(np.arange(T // 64), 64).astype(np.float32), np.tile(np.arange(64), T // 64).astype(np.float32)
    ax = np.float32(10000.0) ** (-np.arange(16, dtype=np.float32) / np.float32(16))
    a = np.concatenate([row[:, None] * ax, col[:, None] * ax], axis=1).T
    put("axial_cos", np.tile(np.cos(a), (4, 1)))
    put("axial_sin", np.tile(np.sin(a), (4, 1)))
    put("tri", (s < t).astype(np.float32))
    put("expert_no", np.arange(N_EXP)[None, :])
    put("block_no", np.arange(N_BLOCKS)[None, :])
    put("token_no", (np.arange(P)[:, None] + P * np.arange(TT)[None, :]))
    return c


def lay_out(inp):
    def fm(a):
        a = np.asarray(a)
        return np.ascontiguousarray(a.T.reshape(-1, P, a.shape[0]).transpose(1, 0, 2))

    arr = {"xT": fm(inp["x"][0]), "memT": fm(inp["mem"][0]), "ctxT": fm(inp["ctx_2"][0])}
    v = np.zeros((P, N_VEC), np.float32)
    for name, k in VECS:
        v[:, VEC_AT[name]:VEC_AT[name] + k] = np.asarray(inp[name]).reshape(k, P).T
    arr["vecs"] = v
    w = np.zeros((NT, P, SLOT), np.float32)
    for t, (name, k0, kc, at, n) in enumerate(WT):
        a = np.asarray(inp[name])[0][k0 * P:(k0 + kc) * P, at:at + n]
        w[t, :, 0:kc * n] = a.reshape(kc, P, n).transpose(1, 0, 2).reshape(P, kc * n)
    arr["wt"] = w
    arr["pos"] = np.ascontiguousarray(np.asarray(inp["positions"])[0])
    arr["wr"] = np.ascontiguousarray(np.asarray(inp["w_router_2"])[0].reshape(DC, P, N_EXP).transpose(1, 0, 2))
    arr["br"] = np.ascontiguousarray(np.asarray(inp["b_router_2"])[0][None, :])
    arr["wgu"] = np.asarray(inp["w_gate_up_2"])[0]
    arr["bgu"] = np.asarray(inp["b_gate_up_2"])[0]
    arr["wdn"] = np.asarray(inp["w_down_2"])[0]
    arr["bdn"] = np.asarray(inp["b_down_2"])[0]
    arr["consts"] = constants()
    return arr


ORDER = ["wt", "xT", "memT", "ctxT", "pos", "vecs", "consts", "wr", "br", "wgu", "bgu", "wdn", "bdn"]
DEBUG = None


def kernel(**inputs):
    import concourse.bacc as bacc
    from concourse.bass_utils import run_bass_kernel_spmd as run

    nc = bacc.Bacc("TRN2", target_bir_lowering=False, num_devices=1)
    arrays = {f"in_{k}": v for k, v in lay_out(inputs).items()}
    args = [nc.dram_tensor(f"in_{k}", arrays[f"in_{k}"].shape, mybir.dt.from_np(arrays[f"in_{k}"].dtype),
                           kind="ExternalInput").ap() for k in ORDER]
    f32, i32 = mybir.dt.float32, mybir.dt.int32
    out = nc.dram_tensor("outT", (P, DC, T), f32, kind="ExternalOutput").ap()
    hrows = nc.dram_tensor("h_rows", (T, D), f32).ap()
    tokof = nc.dram_tensor("token_of_row", (N_ROWS, 1), i32).ap()
    yrows = nc.dram_tensor("y_rows", (N_ROWS, D), f32).ap()
    blk = nc.dram_tensor("block_table", (1, 64), i32).ap()
    if DEBUG:
        build(nc, *args, out, hrows, tokof, yrows, blk, dbg=out, stop=DEBUG)
    else:
        build(nc, *args, out, hrows, tokof, yrows, blk)
    r = run(nc, [arrays], core_ids=[0])
    got = np.asarray(r.results[0]["outT"])
    return np.ascontiguousarray(got.transpose(1, 0, 2).reshape(D, T).T)[None]
```

```python
import numpy as np
import concourse.bass as bass
from concourse import mybir
from contextlib import ExitStack

P = 128
D = 1024
DC = D // P
T = 512
TT = T // P
M = 256
TA = T + M
AC = TA // P
DFF = 4096
HEADS1, DH1 = 8, 64
EPS = 1e-6
NEG = -1e30
SLOT = 2048
RING = 5
N_EXP, TOPK = 32, 4
N_BLOCKS = T * TOPK // P + N_EXP
YBUF = 8
N_ROWS = (N_BLOCKS + 1) * P
MT = 24
MC = 1024
LEVELS = 7

C_Q, C_KV, C_KR, C_HQ, C_ZF, C_ZB, C_V, C_G, C_P7, C_P8 = 0, 768, 1024, 1088, 2112, 3136, 4160, 5184, 6208, 7232

VECS = [("g_pre_mix", 8), ("g_mem", 8), ("conv_w", 6), ("g_attn_out", 4), ("g_conv_out", 2), ("g_xattn_out", 2),
        ("g_post_mix", 8), ("g_pre_mlp", 8), ("g_post_mlp", 8), ("c_2", 8), ("c_ctx_2", 8), ("b_mod_2", 48),
        ("norm_mix_g_2", 8), ("mla_q_norm_g_2", 6), ("mla_kv_norm_g_2", 2), ("hg_lb_logits_2", 32),
        ("hg_norm_g_2", 1), ("norm_ffn_g_2", 8), ("final_norm_g_2", 8)]
VEC_AT = {}
_n = 0
for _name, _k in VECS:
    VEC_AT[_name] = _n
    _n += _k
N_VEC = _n

CONSTS = [("ident", P), ("ones", P), ("rot", P), ("band", T), ("levels", 14 * P // 8), ("diagonal", P // 4), ("reset", TA),
          ("inv_freq", 1), ("rot_sign", 1), ("axial_cos", T), ("axial_sin", T), ("tri", P), ("expert_no", N_EXP),
          ("block_no", N_BLOCKS), ("token_no", TT), ("row_no", P)]
CONST_AT = {}
_n = 0
for _name, _k in CONSTS:
    CONST_AT[_name] = _n
    _n += _k
N_CONST = _n


def weight_tiles():
    out = []

    def cols(name, at, n, kc=DC, k0=0):
        out.append((name, k0, kc, [(at, n)], n))

    for i in range(10):
        cols("w_in", 256 * i, 256)
    for i in range(2):
        cols("w_mem_kv", 256 * i, 256)
    for i in range(12):
        for k in range(2):
            cols("w_mod_2", 512 * i, 512, 4, 4 * k)
    for i in range(4):
        cols("w_out", 256 * i, 256)
    for i in range(16):
        cols("w_up", 256 * i, 256)
    for i in range(4):
        for k in range(4):
            cols("w_down", 256 * i, 256, DC, DC * k)
    for i in range(4):
        cols("w_in_2", 256 * i, 256)
    cols("w_in_2", C_KR, 64)
    for g in range(4):
        cols("w_q_b_2", 384 * g, 192, 6)
        cols("w_q_b_2", 384 * g + 192, 192, 6)
        cols("w_kv_b_2", 512 * g, 512, 2)
    for n in range(8):
        for parts in ((C_HQ, C_ZF), (C_ZB, C_G), (C_V, C_P7), (C_P8,)):
            out.append(("w_in_2", 0, DC, [(at + P * n, P) for at in parts], P * len(parts)))
    for i in range(4):
        cols("w_out_2", 256 * i, 256)
    return out


WT = weight_tiles()
NT = len(WT)


def build(nc, wt, xT, memT, ctxT, pos, vecs, consts, wr, br, wgu, bgu, wdn, bdn, out, hrows, tokof, yrows, blk_dram, dbg=None, stop=None):
    fp32, i32, u8 = mybir.dt.float32, mybir.dt.int32, mybir.dt.uint8
    ALU, ACT, AX = mybir.AluOpType, mybir.ActivationFunctionType, mybir.AxisListType
    F = ACT

    ctx = ExitStack()
    with ctx:
        def sb(name, cols, dt=fp32):
            return ctx.enter_context(nc.sbuf_tensor(name, [P, cols], dt))

        def sem(name):
            return ctx.enter_context(nc.semaphore(name))

        def v3(ap, n):
            return ap.rearrange("p (a b) -> p a b", a=n)

        ring = sb("ring", RING * SLOT)
        x = v3(sb("x", DC * T)[:, :], DC)
        cst = sb("cst", N_CONST)
        vec = sb("vec", N_VEC)
        sq = v3(sb("sq", 2 * T)[:, :], 2)
        ms = sb("ms", T)
        rstd = sb("rstd", T)
        mod = sb("mod", 96)
        small = sb("small", 160)
        cs = sb("conditions", 16)[:, :]
        zeros = sb("zeros", 512)[:, :]
        arena = sb("arena", 32000)
        G = ctx.enter_context(nc.psum_tensor("product_banks", [P, 2048], fp32))
        jb = [G[:, 512 * i:512 * i + 512] for i in range(4)]
        S = ctx.enter_context(nc.psum_tensor("score_banks", [P, 1024], fp32))
        PT = ctx.enter_context(nc.psum_tensor("turn_bank", [P, 512], fp32))
        PO = ctx.enter_context(nc.psum_tensor("out_bank", [P, 512], fp32))
        LB = [S[:, 0:512], S[:, 512:1024]]

        def const(name):
            k = dict(CONSTS)[name]
            return cst[:, CONST_AT[name]:CONST_AT[name] + k]

        def vcol(name, i=0, n=1):
            return vec[:, VEC_AT[name] + i:VEC_AT[name] + i + n]

        ident, ones, rot = const("ident"), const("ones"), const("rot")
        level_masks = v3(const("levels").bitcast(u8), 14)
        diagonal = const("diagonal").bitcast(u8)

        class Area:
            def __init__(self, at=0):
                self.at = at

            def take(self, cols, n=None):
                a = arena[:, self.at:self.at + cols]
                self.at += cols
                assert self.at <= 32000, self.at
                return v3(a, n) if n else a

        A = Area()
        h = A.take(DC * T, DC)
        mark_h = A.at
        q1 = A.take(4 * T, 4)
        k1 = A.take(4 * T, 4)
        v1 = A.take(TT * 512, TT)
        cb, cc, cu = A.take(2 * T, 2), A.take(2 * T, 2), A.take(2 * T, 2)
        qx = A.take(2 * T, 2)
        mem = A.take(DC * M, DC)
        hm = A.take(DC * M, DC)
        km = A.take(2 * M, 2)
        vm = A.take(2 * M, 2)
        cosT, sinT, ang, trn = A.take(T), A.take(T), A.take(T), A.take(T)
        probs1, probsT1, masked = A.take(2 * TA, 2), A.take(TA), A.take(T)
        yconv = A.take(2 * T, 2)
        modrow = A.take(6 * D)
        yatt = mem.rearrange("p a b -> p (a b)")
        yatt = v3(yatt[:, 0:4 * T], 4)
        yxa = v3(hm.rearrange("p a b -> p (a b)")[:, 0:2 * T], 2)
        A = Area(mark_h)
        mix_out = A.take(DC * T, DC)
        ffn = A.take(DFF // P * T, DFF // P)
        A = Area()
        ha = A.take(DC * TA, DC)
        ymla = A.take(DC * T, DC)
        mark2 = A.at
        cx = Area(32000 - DC * M).take(DC * M, DC)
        A = Area(mark2)
        qin = A.take(6 * T, 6)
        ckv = A.take(2 * TA, 2)
        kr = A.take(TA)
        qn = A.take(4 * T, 4)
        qr = A.take(4 * T, 4)
        kn = A.take(4 * TA, 4)
        vv = A.take(2 * AC * 256, 2 * AC)
        probs2, probsT2 = A.take(2 * TA, 2), A.take(TA)
        tmp2 = A.take(T)
        assert A.at <= 32000 - DC * M
        A = Area(mark2)
        hq = A.take(2 * T, 2)
        hg = A.take(2 * T, 2)
        s7 = A.take(2 * T, 2)
        s8 = A.take(2 * T, 2)
        zs = A.take(4 * TA, 4)
        hv = A.take(AC * 256, AC)
        lnA = A.take(TA)
        kk = A.take(2 * TA, 2)
        cum = A.take(2 * TA, 2)
        qq = A.take(T)
        dlt = A.take(2 * TA, 2)
        E = A.take(2 * TA, 2)
        X = A.take(2 * T, 2)
        qe = A.take(2 * T, 2)
        kT = A.take(TA, AC)
        St = A.take(2 * 5 * P, 10)
        At = A.take(T)
        osb = A.take(T)
        el = A.take(12, 2)
        A = Area(mark2)
        mout2 = A.take(DC * T, DC)

        mw = arena[:, 0:MT * MC].rearrange("p (a b) -> p a b", a=MT)
        A = Area(MT * MC)
        aT = A.take(1024, 8)
        brow = A.take(3072)
        lg = A.take(TT * N_EXP, TT)
        top8 = A.take(TT * 8, TT)
        idx8 = A.take(TT * 8, TT)
        idxf = A.take(TT * 4, TT)
        hot = A.take(TT * 4 * N_EXP)
        hot2 = A.take(TT * 4 * N_EXP)
        member = A.take(TT * N_EXP, TT)
        cmpb = arena[:, 0:N_BLOCKS * N_EXP]
        blocks_of = A.take(N_EXP)
        block_end = A.take(N_EXP)
        first_row = A.take(N_EXP)
        rank = A.take(TT * N_EXP, TT)
        destf = A.take(16)
        desti = A.take(16)
        prob = A.take(16)
        tokno = A.take(TT)
        tab = A.take(N_BLOCKS + 16)
        block_expert = A.take(N_BLOCKS)
        wrs = A.take(DC * N_EXP, DC)
        brs = A.take(N_EXP)
        idx_in = A.take(1)
        held = A.take(1)
        rg = ring[:, :]
        h3 = v3(rg[:, 0:4096], DC)
        hr = v3(rg[:, 4096:8192], TT)
        biasb = rg[:, 0:3072]
        tbuf = rg[:, 3072:4096]
        glu = rg[:, 4096:4608]
        lin = rg[:, 4608:5120]
        sig = rg[:, 5120:5632]
        actb = rg[:, 5632:6656]
        yb = rg[:, 6656:7680]
        xg = rg[:, 7680:8704]
        xTb = v3(rg[:, 8704:9728], 8)
        select = A.take(TT * P, TT)
        acc = arena[:, 0:4096].rearrange("p (a b) -> p a b", a=TT)
        yg = arena[:, 14336:14336 + YBUF * D].rearrange("p (a b) -> p a b", a=YBUF)
        yT = arena[:, 6144:10240].rearrange("p (a b) -> p a b", a=DC)
        fin = arena[:, 10240:14336].rearrange("p (a b) -> p a b", a=DC)

        s_const = sem("constants_loaded")
        s_in = sem("activations_loaded")
        s_pos = sem("positions_loaded")
        s_tok = sem("side_tokens_loaded")
        s_slot = [sem(f"weights_loaded{i}") for i in range(RING)]
        s_pair = sem("pair_ready")
        s_evac = sem("pair_evacuated")
        s_sq = sem("squares_ready")
        s_mm = sem("squares_summed")
        s_ms = sem("mean_squares_ready")
        s_rt = sem("roots_ready")
        s_norm = sem("norm_written")
        s_rot_in = sem("rope_input_ready")
        s_rot = sem("rope_turned")
        s_rope = sem("rope_written")
        s_sc = sem("scores_ready")
        s_max = sem("max_ready")
        s_exp = sem("exps_ready")
        s_prob = sem("probs_ready")
        s_tr = sem("probs_turned")
        s_trc = sem("turned_copied")
        s_pv = sem("values_summed")
        s_out = sem("heads_written")
        s_vec = sem("vector_step")
        s_act = sem("scalar_step")
        s_ang = sem("angles_ready")
        s_sin = sem("sines_ready")
        s_ffn = sem("ffn_squared")
        s_silu = sem("conditions_ready")
        s_silc = sem("conditions_exp")
        s_res = sem("residual_ready")
        s_modt = sem("modulation_turned")
        s_modr = sem("modulation_ready")
        s_lb = sem("bounds_max_ready")
        s_lbe = sem("bounds_exp_ready")
        s_f = sem("forget_clamped")
        s_ln = sem("forget_logged")
        s_cum = sem("decay_summed")
        s_ec = sem("decay_exps")
        s_kd = sem("keys_decayed")
        s_kt = sem("keys_turned")
        s_ktc = sem("turned_keys_copied")
        s_ds = sem("state_terms")
        s_st = sem("states_ready")
        s_d = sem("level_difference")
        s_e = sem("level_exps")
        s_x = sem("level_operand")
        s_p = sem("level_products")
        s_at = sem("weights_gathered")
        s_o = sem("outputs_summed")
        s_osb = sem("outputs_copied")
        s_hg = sem("head_merged")
        s_sil = sem("silu_factor")
        s_end = sem("output_stored")
        s_route_w = sem("router_weights_loaded")
        s_zero = sem("zeros_ready")
        s_held = sem("waits_held")
        s_yclear = sem("row_tables_cleared")
        s_lgp = sem("logit_products")
        s_top = sem("top_maxima")
        s_tope = sem("top_exps")
        s_mem = sem("membership_ready")
        s_rank = sem("ranks_ready")
        s_cnt = sem("expert_counts_ready")
        s_sel = sem("first_block_selected")
        s_dest = sem("rows_assigned")
        s_tab = sem("block_table_ready")
        s_hT = sem("h_rows_turned")
        s_hc = sem("h_rows_copied")
        s_hst = sem("h_rows_stored")
        s_scat = sem("row_tokens_scattered")
        s_w = [sem(f"expert_tile_loaded{i}") for i in range(MT)]
        s_used = sem("expert_tiles_used")
        s_brow = sem("bias_rows_loaded")
        s_bb = sem("bias_broadcast")
        s_tk = sem("block_tokens_loaded")
        s_ga = sem("block_inputs_gathered")
        s_xtp = sem("inputs_turned")
        s_xtc = sem("turned_inputs_copied")
        s_glu = sem("glu_ready")
        s_sig = sem("sigmoid_ready")
        s_lg = sem("gated_linear_ready")
        s_actr = sem("activation_ready")
        s_atp = sem("activation_turned")
        s_atc = sem("turned_activation_copied")
        s_y = sem("expert_rows_ready")
        s_yst = sem("expert_rows_stored")
        s_vl = sem("vector_loop_step")
        s_yg = [sem(f"token_rows_gathered{i}") for i in range(YBUF)]
        s_acc = sem("token_sum_ready")
        s_tT = sem("token_sums_turned")
        s_tTc = sem("turned_sums_copied")

        def tile_ap(t):
            _, _, kc, _, n = WT[t]
            s = t % RING
            return v3(ring[:, s * SLOT:s * SLOT + kc * n], kc)

        pairs = []
        stages = {}
        state = {"tile": 0}

        def next_tile():
            state["tile"] += 1
            return state["tile"] - 1

        def pair(stage, groups, evacs):
            pairs.append((groups, evacs))
            stages.setdefault(stage, [len(pairs) - 1, len(pairs)])[1] = len(pairs)

        def feature_pair(stage, tiles, src, width, dst, func=F.Copy, scale=1.0, bias=None, rows=(P, P)):
            groups, evacs = [], []
            at = 0
            for m in range(len(dst)):
                mm = []
                for t in tiles:
                    w = tile_ap(t)
                    k0 = WT[t][1]
                    for k in range(WT[t][2]):
                        mm.append((t, w[:, k, at:at + rows[m]], src[:, (k0 + k), 0:width] if width else src[:, k0 + k, :]))
                groups.append([(mm, rows[m], 0, width)])
                evacs.append((dst[m], func, scale, bias[m] if bias else 0.0, rows[m], width))
                at += rows[m]
            pair(stage, groups, evacs)

        def token_pair(stage, t, src, tiles, wcols, n, dst):
            groups, evacs = [], []
            for i, j in enumerate(tiles):
                w = tile_ap(t)
                mm = [(t, src[:, k, P * j:P * j + P], wcols(w, k)) for k in range(WT[t][2])]
                groups.append([(mm, P, 0, n)])
                evacs.append((dst[i], F.Copy, 1.0, 0.0, P, n))
            pair(stage, groups, evacs)

        plain = lambda w, k: w[:, k, :]
        for i in range(10):
            t = next_tile()
            if i < 4:
                to = q1 if i < 2 else k1
                feature_pair("in1", [t], h, T, [to[:, 2 * (i % 2), :], to[:, 2 * (i % 2) + 1, :]])
            elif i < 6:
                for j in (0, 2):
                    token_pair("in1", t, h, [j, j + 1], plain, 256,
                               [v1[:, j, 256 * (i - 4):256 * (i - 3)], v1[:, j + 1, 256 * (i - 4):256 * (i - 3)]])
            else:
                to = (cb, cc, cu, qx)[i - 6]
                feature_pair("side1", [t], h, T, [to[:, 0, :], to[:, 1, :]])
        feature_pair("side1", [next_tile()], hm, M, [km[:, 0, :], km[:, 1, :]])
        token_pair("side1", next_tile(), hm, [0, 1], plain, 256, [vm[:, 0, :], vm[:, 1, :]])
        modv = v3(mod[:, :], 48)
        for i in range(6):
            groups, evacs = [], []
            for m in range(2):
                mm = []
                for t in (next_tile(), next_tile()):
                    w = tile_ap(t)
                    mm += [(t, v3(cs, 8)[:, WT[t][1] + k, :], w[:, k, :]) for k in range(WT[t][2])]
                groups.append([(mm, 2, 0, 512)])
                evacs.append((modrow[0:2, 512 * (2 * i + m):512 * (2 * i + m + 1)], F.Copy, 1.0, 0.0, 2, 512))
            pair("mod", groups, evacs)
        for i in range(4):
            feature_pair("out1", [next_tile()], h, T, [mix_out[:, 2 * i + m, :] for m in range(2)])
        for i in range(16):
            feature_pair("up", [next_tile()], h, T, [ffn[:, 2 * i + m, :] for m in range(2)], F.Relu)
        for i in range(4):
            feature_pair("down", [next_tile() for _ in range(4)], ffn, T, [mix_out[:, 2 * i + m, :] for m in range(2)])
        hctx = ha[:, :, T:TA]
        for i in range(3):
            feature_pair("in2q", [next_tile()], ha, T, [qin[:, 2 * i + m, :] for m in range(2)])
        t = next_tile()
        feature_pair("in2", [t], ha, T, [ckv[:, m, 0:T] for m in range(2)])
        feature_pair("in2", [t], hctx, M, [ckv[:, m, T:TA] for m in range(2)])
        t = next_tile()
        feature_pair("in2", [t], ha, T, [kr[0:64, 0:T]], rows=(64,))
        feature_pair("in2", [t], hctx, M, [kr[0:64, T:TA]], rows=(64,))
        for g in range(4):
            s0 = 2 * (g % 2)
            for m in range(2):
                feature_pair(f"mla{g}", [next_tile()], qin, T, [qn[:, s0 + m, :], qr[0:64, s0 + m, :]], rows=(P, 64))
            t = next_tile()
            w = tile_ap(t)
            for a, b in ((0, T), (T, TA)):
                groups = [[([(t, w[:, k, 256 * m:256 * m + P], ckv[:, k, a:b]) for k in range(2)], P, 0, b - a)] for m in range(2)]
                pair(f"mla{g}", groups, [(kn[:, s0 + m, a:b], F.Copy, 1.0, 0.0, P, b - a) for m in range(2)])
            vcols = lambda w, k: w[:, k, :].rearrange("p (h c) -> p h c", h=2)[:, :, P:2 * P]
            for j in range(0, AC, 2):
                token_pair(f"mla{g}", t, ckv, [j, j + 1], vcols, 256, [vv[:, 3 * s0 + j, :], vv[:, 3 * s0 + j + 1, :]])
        def head_part(t, part, src, width):
            w = tile_ap(t)
            return [([(t, w[:, k, P * part:P * part + P], src[:, k, 0:width]) for k in range(DC)], P, 0, width)]

        def head_values(t, tiles):
            w = tile_ap(t)
            return [([(t, ha[:, k, P * j:P * j + P], w[:, k, 0:P]) for k in range(DC)], P, P * i, P) for i, j in enumerate(tiles)]

        for n in range(8):
            st, m = f"hg{n}", n % 2
            ta, tb, tc, td = (next_tile() for _ in range(4))

            def to(dst, func=F.Copy, cols=T):
                return (dst, func, 1.0, 0.0, P, cols)

            pair(st, [head_part(ta, 0, ha, T), head_part(ta, 1, ha, T)], [to(hq[:, m, :]), to(zs[:, m, 0:T], F.Sigmoid)])
            pair(st, [head_part(tb, 0, ha, T), head_part(tb, 1, ha, T)], [to(zs[:, 2 + m, 0:T], F.Sigmoid), to(hg[:, m, :])])
            pair(st, [head_part(ta, 1, hctx, M), head_part(tb, 0, hctx, M)],
                 [to(zs[:, m, T:TA], F.Sigmoid, M), to(zs[:, 2 + m, T:TA], F.Sigmoid, M)])
            pair(st, [head_values(tc, [0, 1, 2, 3]), head_values(tc, [4, 5])],
                 [to(hv[:, 0:4, P * m:P * m + P]), to(hv[:, 4:6, P * m:P * m + P], F.Copy, M)])
            pair(st, [head_part(tc, 1, ha, T), head_part(td, 0, ha, T)], [to(s7[:, m, :], F.Sigmoid), to(s8[:, m, :], F.Sigmoid)])
        for i in range(4):
            feature_pair("out2", [next_tile()], ymla, T, [mout2[:, 2 * i + m, :] for m in range(2)])
        assert state["tile"] == NT
        last_pair_of = {}
        for n, (groups, _) in enumerate(pairs):
            for parts in groups:
                for mm, _, _, _ in parts:
                    for t, _, _ in mm:
                        last_pair_of[t] = n

        def products_in(n):
            return sum(len(mm) for parts in pairs[n][0] for mm, _, _, _ in parts)

        def filled(stage, weights, i):
            a, b = stages[stage]
            total = sum(products_in(n) for n in range(a, b))
            done = total * sum(weights[:i + 1]) // sum(weights)
            n, left = a, done
            while n < b and products_in(n) <= left:
                left -= products_in(n)
                n += 1
            return done, n

        UNIT8, UNIT16, UNIT32 = [1] * 16, [1] * 32, [1] * 64
        HEAD_SLOTS = [7, 1, 5, 1] + [1] * 14 + [2]

        NORMS = [("pre_mix", x, 8, T), ("mem", mem, 8, M), ("attn", yatt, 4, T), ("conv", yconv, 2, T),
                 ("xattn", yxa, 2, T), ("post_mix", mix_out, 8, T), ("pre_mlp", x, 8, T), ("post_mlp", mix_out, 8, T),
                 ("mix2", x, 8, T), ("ctx", cx, 8, M), ("qin", qin, 6, T), ("ckv_lat", ckv, 2, T),
                 ("ckv_ctx", ckv[:, :, T:TA], 2, M)]
        NORMS += [(f"head{n}", osb.unsqueeze(1), 1, T) for n in range(8)]
        NORMS += [("ffn2", x, 8, T), ("final", x, 8, T)]
        NI = {n[0]: i for i, n in enumerate(NORMS)}
        chunk0 = [sum(n[2] for n in NORMS[:i]) for i in range(len(NORMS))]

        APPLIED = [n for n in NORMS if n[0] not in ("post_mix", "post_mlp") and not n[0].startswith("head")]

        def normed(name, chunks=None):
            at = [n[0] for n in APPLIED].index(name)
            return sum(n[2] for n in APPLIED[:at]) + (APPLIED[at][2] if chunks is None else chunks)

        UNITS = []
        for hd in range(HEADS1):
            r = slice(64 * (hd % 2), 64 * (hd % 2) + 64)
            for i in range(TT):
                nk = P * (i + 1)
                UNITS.append(dict(sc=[[(q1[r, hd // 2, P * i:P * i + P], k1[r, hd // 2, 0:nk], 0, nk)]], nk=nk,
                                  v=[v1[:, j, P * (hd // 2):P * (hd // 2) + P] for j in range(i + 1)], rows=r,
                                  dst=yatt[r, hd // 2, P * i:P * i + P], scale=DH1 ** -0.5,
                                  mask=const("band")[:, T - P - P * i:T - P - P * i + nk], pr=probs1, pt=probsT1))
        U_X = len(UNITS)
        for hd in range(4):
            r = slice(64 * (hd % 2), 64 * (hd % 2) + 64)
            for i in range(TT):
                UNITS.append(dict(sc=[[(qx[r, hd // 2, P * i:P * i + P], km[r, hd // 2, :], 0, M)]], nk=M,
                                  v=[vm[:, j, P * (hd // 2):P * (hd // 2) + P] for j in range(2)], rows=r,
                                  dst=yxa[r, hd // 2, P * i:P * i + P], scale=64 ** -0.5, mask=None, pr=probs1, pt=probsT1))
        U_M = len(UNITS)
        for hd in range(8):
            m = hd % 4
            for i in range(TT):
                qs = slice(P * i, P * i + P)
                UNITS.append(dict(sc=[[(qn[:, m, qs], kn[:, m, a:b], a, b), (qr[0:64, m, qs], kr[0:64, a:b], a, b)]
                                      for a, b in ((0, T), (T, TA))], nk=TA,
                                  v=[vv[:, AC * (m // 2) + j, P * (m % 2):P * (m % 2) + P] for j in range(AC)], rows=slice(0, P),
                                  dst=ymla[:, hd, qs], scale=192 ** -0.5, mask=None, pr=probs2, pt=probsT2))
        turns0 = []
        n = 0
        for u in UNITS:
            turns0.append(n)
            n += (len(u["v"]) + 3) // 4
        ROPES = [(q1[:, c, :], cosT, sinT, P) for c in range(4)] + [(k1[:, c, :], cosT, sinT, P) for c in range(4)]
        ac_, as_ = const("axial_cos"), const("axial_sin")
        ROPES += [(kr[0:64, 0:T], ac_[0:64, :], as_[0:64, :], 64)]
        for g in range(4):
            ROPES += [(qr[0:64, 2 * (g % 2) + m, :], ac_[0:64, :], as_[0:64, :], 64) for m in range(2)]

        level_half = [P >> (i + 1) for i in range(LEVELS)]
        SEQ = [[4, 5, 0, 1, 2, 3], [5, 4, 3, 2, 1, 0]]

        tab_i = tab.bitcast(i32)
        desti_u = desti.bitcast(mybir.dt.uint32)
        block = ctx.enter_context(nc.Block())

        @block.sync
        def _(sp):
            sp.dma_start(cst[:, :], consts).then_inc(s_const, 16)
            sp.dma_start(vec[:, :], vecs).then_inc(s_const, 16)
            sp.dma_start(x, xT).then_inc(s_in, 16)
            for t in range(NT if stop != "x1" else 72):
                if t >= RING:
                    sp.wait_ge(s_pair, last_pair_of[t - RING] + 1)
                _, _, kc, _, n = WT[t]
                s = t % RING
                sp.dma_start(ring[:, s * SLOT:s * SLOT + kc * n], wt[t, :, 0:kc * n]).then_inc(s_slot[s], 16)
            if dbg is None:
                sp.wait_ge(s_hg, 8)
                sp.dma_start(wrs, wr).then_inc(s_route_w, 16)
                sp.dma_start(brs[0:1, :], br).then_inc(s_route_w, 16)
                for i in range(TT):
                    sp.wait_ge(s_hc, i + 1)
                    sp.dma_start(hrows[P * i:P * i + P, :], hr[:, i, :]).then_inc(s_hst, 16)
                sp.wait_ge(s_tab, 1)
                nb = sp.value_load(tab_i[0:1, N_BLOCKS:N_BLOCKS + 1], min_val=T * TOPK // P, max_val=N_BLOCKS)

                def load_expert(e, b):
                    if b is not None:
                        sp.wait_ge(s_bb, b)
                    sp.dma_start(brow[0:1, 0:2048], bgu[bass.ds(e, 1), :]).then_inc(s_brow, 16)
                    sp.dma_start(brow[0:1, 2048:3072], bdn[bass.ds(e, 1), :]).then_inc(s_brow, 16)
                    for t in range(MT):
                        if b is not None:
                            sp.wait_ge(s_used, b * MT + (t + 1 - MT))
                        if t < 16:
                            k, hf = t % 8, t // 8
                            src = wgu[bass.ds(e, 1), P * k:P * k + P, MC * hf:MC * hf + MC]
                        else:
                            k = t - 16
                            src = wdn[bass.ds(e, 1), P * k:P * k + P, :]
                        sp.dma_start(mw[:, t, :], src.rearrange("a p n -> (a p) n")).then_inc(s_w[t], 16)

                load_expert(sp.value_load(tab_i[0:1, 0:1], min_val=0, max_val=N_EXP - 1), None)
                with sp.Fori(1, nb) as b:
                    load_expert(sp.value_load(tab_i[0:1, bass.ds(b, 1)], min_val=0, max_val=N_EXP - 1), b)
                for c in range(DC):
                    sp.wait_ge(s_norm, normed("final", c + 1))
                    sp.dma_start(out[:, c, :], fin[:, c, :]).then_inc(s_end, 16)
                sp.wait_ge(s_end, 16 * DC)
            if dbg is not None:
                sp.wait_ge(s_hg if stop == "hg" else s_res, 1 if stop == "x1" else 8 if stop == "hg" else 2)
                src = x if stop != "hg" else ymla
                sp.dma_start(dbg, src).then_inc(s_end, 16)
                sp.wait_ge(s_end, 16)

        @block.gpsimd
        def _(gp):
            gp.dma_start(ang.bitcast(i32), pos.partition_broadcast(P)).then_inc(s_pos, 16)
            gp.dma_start(mem, memT).then_inc(s_tok, 16)
            gp.memset(zeros, 0.0).then_inc(s_zero, 1)
            gp.wait_ge(s_zero, 1)
            gp.dma_start(tokof.rearrange("(p n) o -> p (n o)", p=P),
                         zeros.bitcast(i32)[:, 0:N_ROWS // P]).then_inc(s_yclear, 16)
            gp.wait_ge(s_res, 1)
            gp.dma_start(cx, ctxT).then_inc(s_tok, 16)
            for n in range(8):
                gp.wait_ge(s_ec, 2 * n + 2)
                for L in range(14):
                    hf, d = level_half[L % LEVELS], L // LEVELS
                    nb = T // (2 * hf)
                    if L >= 2:
                        gp.wait_ge(s_e, 14 * n + L - 1)
                    c3 = cum[:, d, 0:T].rearrange("p (b s) -> p b s", s=2 * hf)
                    ref = c3[:, :, hf - 1:hf] if d == 0 else c3[:, :, hf:hf + 1]
                    gp.tensor_tensor(dlt[:, L % 2, 0:T].rearrange("p (b s) -> p b s", s=2 * hf), c3,
                                     ref.broadcast_to([P, nb, 2 * hf]), ALU.subtract).then_inc(s_d, 1)
            if dbg is not None:
                return
            gp.wait_ge(s_hg, 8)
            gp.wait_ge(s_yclear, 16)
            gp.wait_ge(s_dest, 1)
            for i in range(TT):
                for k in range(TOPK):
                    j = TOPK * i + k
                    gp.indirect_dma_start(tokof, bass.IndirectOffsetOnAxis(desti_u[:, j:j + 1], 0),
                                          tokno.bitcast(i32)[:, i:i + 1], None).then_inc(s_scat, 16)
            gp.wait_ge(s_scat, 16 * TT * TOPK)
            gp.wait_ge(s_hst, 16 * TT)
            gp.wait_ge(s_tab, 1)
            nb = gp.value_load(tab_i[0:1, N_BLOCKS:N_BLOCKS + 1], min_val=T * TOPK // P, max_val=N_BLOCKS)

            gp.memset(held[0:1, :], 0.0).then_inc(s_held, 1)

            def hold_waits(n):
                gp.wait_ge(s_held, n)
                gp.tensor_tensor(held[0:1, :], zeros[0:1, 0:1], zeros[0:1, 0:1], ALU.add).then_inc(s_held, 1)

            def gather(row, count, holds=None):
                gp.dma_start(idx_in.bitcast(i32), tokof[bass.ds(row, P), :]).then_inc(s_tk, 16)
                gp.wait_ge(s_tk, count)
                if holds is not None:
                    hold_waits(holds)
                gp.indirect_dma_start(xg, None, hrows, bass.IndirectOffsetOnAxis(idx_in.bitcast(mybir.dt.uint32), 0)).then_inc(s_ga, 16)

            with gp.Fori(0, nb) as b:
                gp.wait_ge(s_brow, b * 32 + 32)
                gp.wait_ge(s_y, b + 1)
                hold_waits(b * 2 + 1)
                gp.partition_broadcast(biasb, brow[0:1, :]).then_inc(s_bb, 1)
                gp.wait_ge(s_xtp, b * 2 + 2)
                gp.wait_ge(s_ga, b * 16)
                gather(b * P + P, b * 16 + 16, b * 2 + 2)
            gp.wait_ge(s_yst, nb * 16 + 32)
            for i in range(TT):
                for k in range(TOPK):
                    j = TOPK * i + k
                    if j == 0:
                        gp.wait_ge(s_used, nb * MT)
                        hold_waits(nb * 2 + 1)
                    if j >= YBUF:
                        gp.wait_ge(s_acc, j - YBUF + 1)
                    gp.indirect_dma_start(yg[:, j % YBUF, :], None, yrows,
                                          bass.IndirectOffsetOnAxis(desti_u[:, j:j + 1], 0)).then_inc(s_yg[j % YBUF], 16)

        @block.tensor
        def _(pe):
            seen = set()

            def product_steps(stage):
                a, b = stages[stage]
                for n in range(a, b):
                    if n >= 2:
                        pe.wait_ge(s_evac, n - 1)
                    left = products_in(n)
                    for m, parts in enumerate(pairs[n][0]):
                        bank = jb[2 * (n % 2) + m]
                        for mm, rows, at, cols in parts:
                            for i, (t, lhsT, rhs) in enumerate(mm):
                                if t not in seen:
                                    seen.add(t)
                                    pe.wait_ge(s_slot[t % RING], 16 * (t // RING + 1))
                                ins = nc.tensor.matmul(bank[0:rows, at:at + cols], lhsT, rhs, start=(i == 0), stop=(i == len(mm) - 1))
                                left -= 1
                                if left == 0:
                                    ins.then_inc(s_pair, 1)
                                yield

            def products(stage, source=None):
                for i, _ in enumerate(product_steps(stage)):
                    if source and i < DC - 1:
                        pe.wait_ge(s_norm, normed(source, i + 2))

            class Filler:
                def __init__(self, stage, weights):
                    self.steps, self.stage, self.weights, self.done = product_steps(stage), stage, weights, 0

                def fill(self, i):
                    upto, _ = filled(self.stage, self.weights, i)
                    while self.done < upto:
                        next(self.steps)
                        self.done += 1
                    if i == len(self.weights) - 1:
                        next(self.steps, None)

            def norm(name):
                n = NI[name]
                _, _, nch, w = NORMS[n]
                for c in range(nch):
                    g = chunk0[n] + c
                    pe.wait_ge(s_sq, g + 1)
                    nc.tensor.matmul(PT[:, 0:w], ones, sq[:, g % 2, 0:w], start=(c == 0), stop=(c == nch - 1)).then_inc(s_mm, 1)

            def rope(r):
                buf, _, _, rows = ROPES[r]
                if r >= 2:
                    pe.wait_ge(s_rope, r - 1)
                pe.wait_ge(s_rot_in, 1)
                nc.tensor.matmul(LB[r % 2][0:rows, :], rot[0:rows, 0:rows], buf, start=True, stop=True).then_inc(s_rot, 1)

            def scores(u):
                U = UNITS[u]
                if u:
                    pe.wait_ge(s_exp, u)
                for grp in U["sc"]:
                    for i, (l, r, a, b) in enumerate(grp):
                        ins = nc.tensor.matmul(S[:, a:b], l, r, start=(i == 0), stop=(i == len(grp) - 1))
                ins.then_inc(s_sc, 1)

            def values(u, fill=None):
                U = UNITS[u]
                pe.wait_ge(s_prob, u + 1)
                nv = len(U["v"])
                pr = U["pr"][:, u % 2, :]
                for g in range((nv + 3) // 4):
                    t = turns0[u] + g
                    if t:
                        pe.wait_ge(s_trc, t)
                    for j in range(4 * g, min(4 * g + 4, nv)):
                        ins = nc.tensor.transpose(PT[:, P * (j % 4):P * (j % 4) + P], pr[:, P * j:P * j + P], ident)
                    ins.then_inc(s_tr, 1)
                if fill:
                    fill()
                if u:
                    pe.wait_ge(s_out, u)
                for g in range((nv + 3) // 4):
                    pe.wait_ge(s_trc, turns0[u] + g + 1)
                    for j in range(4 * g, min(4 * g + 4, nv)):
                        ins = nc.tensor.matmul(PO[:, 0:P], U["v"][j], U["pt"][:, P * j:P * j + P], start=(j == 0), stop=(j == nv - 1))
                ins.then_inc(s_pv, 1)

            def attention(a, b, filler=None):
                scores(a)
                for u in range(a, b):
                    if u + 1 < b:
                        scores(u + 1)
                    if filler:
                        filler.fill(2 * (u - a))
                    values(u, (lambda: filler.fill(2 * (u - a) + 1)) if filler else None)

            pe.wait_ge(s_const, 32)
            norm("pre_mix")
            norm("mem")
            pe.wait_ge(s_norm, normed("pre_mix", 1))
            products("in1", "pre_mix")
            pe.wait_ge(s_evac, stages["in1"][1])
            for r in range(8):
                rope(r)
            pe.wait_ge(s_rope, 8)
            pe.wait_ge(s_norm, normed("mem"))
            attention(0, U_X, Filler("side1", UNIT32))
            pe.wait_ge(s_evac, stages["side1"][1])
            pe.wait_ge(s_silu, 1)
            attention(U_X, U_M, Filler("mod", UNIT16))
            pe.wait_ge(s_evac, stages["mod"][1])
            for j in range(48):
                ins = nc.tensor.transpose(PT[:, 2 * j:2 * j + 2], modrow[0:2, P * j:P * j + P], ident[0:2, 0:2])
            ins.then_inc(s_modt, 1)
            pe.wait_ge(s_modr, 1)
            norm("attn")
            norm("conv")
            norm("xattn")
            pe.wait_ge(s_norm, normed("xattn"))
            products("out1")
            norm("post_mix")
            norm("pre_mlp")
            pe.wait_ge(s_norm, normed("pre_mlp", 1))
            products("up", "pre_mlp")
            pe.wait_ge(s_ffn, 16)
            products("down")
            norm("post_mlp")
            if stop == "x1":
                return
            norm("mix2")
            pe.wait_ge(s_norm, normed("mix2", 1))
            products("in2q", "mix2")
            norm("ctx")
            pe.wait_ge(s_norm, normed("ctx"))
            products("in2")
            norm("qin")
            norm("ckv_lat")
            norm("ckv_ctx")
            pe.wait_ge(s_evac, stages["in2"][1])
            rope(8)
            pe.wait_ge(s_norm, normed("ckv_ctx"))
            products("mla0")
            for g in range(4):
                pe.wait_ge(s_evac, stages[f"mla{g}"][1])
                for m in range(2):
                    rope(9 + 2 * g + m)
                pe.wait_ge(s_rope, 11 + 2 * g)
                attention(U_M + 8 * g, U_M + 8 * g + 8, Filler(f"mla{g + 1}", UNIT8) if g < 3 else None)
            products("hg0")
            for n in range(8):
                m = n % 2
                filler = Filler(f"hg{n + 1}", HEAD_SLOTS) if n < 7 else None

                def fill(i):
                    if filler:
                        filler.fill(i)

                pe.wait_ge(s_evac, stages[f"hg{n}"][1])
                for d in range(2):
                    fill(2 * d)
                    pe.wait_ge(s_kd, 2 * n + d + 1)
                    for c in range(AC):
                        ins = nc.tensor.transpose(S[:, P * c:P * c + P], E[:, d, P * c:P * c + P], ident)
                    ins.then_inc(s_kt, 1)
                    fill(2 * d + 1)
                    pe.wait_ge(s_ktc, 2 * n + d + 1)
                    for j in range(5):
                        c = SEQ[d][j]
                        dst = PT[:, P * j:P * j + P] if j < 4 else LB[1][:, 256:384]
                        ins = nc.tensor.matmul(dst, kT[:, c, :], hv[:, c, P * m:P * m + P], start=True, stop=True)
                    ins.then_inc(s_ds, 1)
                    pe.wait_ge(s_st, 2 * n + d + 1)
                for L in range(15):
                    l = 15 * n + L
                    pe.wait_ge(s_x, l + 1)
                    if l >= 2:
                        pe.wait_ge(s_at, l - 1)
                    for c in range(TT):
                        cs_ = slice(P * c, P * c + P)
                        to = LB[L % 2][:, cs_]
                        if L < 14:
                            hf = level_half[L % LEVELS]
                            half = X[:, L % 2, cs_].rearrange("p (b s) -> p b s", s=2 * hf)
                            half = half[:, :, hf:2 * hf] if L < LEVELS else half[:, :, 0:hf]
                            ins = nc.tensor.matmul(LB[L % 2][:, 64 * c:64 * c + 64], X[:, L % 2, cs_], half, start=True, stop=True)
                        else:
                            nc.tensor.matmul(to, kk[:, 0, cs_], qq[:, cs_], start=True, stop=False)
                            ins = nc.tensor.matmul(to, kk[:, 1, cs_], qq[:, cs_], start=False, stop=True)
                    ins.then_inc(s_p, 1)
                    if L < 14:
                        fill(4 + L)
                pe.wait_ge(s_at, 15 * n + 15)
                for c in range(TT):
                    cs_ = slice(P * c, P * c + P)
                    nc.tensor.matmul(PO[:, cs_], St[:, 1 + c, :], qe[:, 0, cs_], start=True, stop=False)
                    nc.tensor.matmul(PO[:, cs_], St[:, 5 + 1 + (3 - c), :], qe[:, 1, cs_], start=False, stop=False)
                    ins = nc.tensor.matmul(PO[:, cs_], hv[:, c, P * m:P * m + P], At[:, cs_], start=False, stop=True)
                ins.then_inc(s_o, 1)
                fill(18)
                norm(f"head{n}")
            pe.wait_ge(s_hg, 8)
            products("out2")
            if dbg is not None:
                return
            norm("ffn2")
            pe.wait_ge(s_norm, normed("ffn2"))
            pe.wait_ge(s_route_w, 32)
            for i in range(TT):
                ts = slice(P * i, P * i + P)
                for c in range(DC):
                    nc.tensor.matmul(PO[:, N_EXP * i:N_EXP * i + N_EXP], h3[:, c, ts], wrs[:, c, :], start=(c == 0), stop=False)
                ins = nc.tensor.matmul(PO[:, N_EXP * i:N_EXP * i + N_EXP], ones[0:1, :], brs[0:1, :], start=False, stop=True)
            ins.then_inc(s_lgp, 1)
            for i in range(TT):
                if i:
                    pe.wait_ge(s_hc, i)
                for c in range(DC):
                    ins = nc.tensor.transpose(S[:, P * c:P * c + P], h3[:, c, P * i:P * i + P], ident)
                ins.then_inc(s_hT, 1)
            pe.wait_ge(s_mem, 1)
            for j in range(TT):
                ins = nc.tensor.matmul(PT[:, 0:N_EXP], ones, member[:, j, :], start=(j == 0), stop=(j == TT - 1))
            ins.then_inc(s_cnt, 1)
            for i in range(TT):
                to = PO[:, 128 + N_EXP * i:128 + N_EXP * i + N_EXP]
                for j in range(i):
                    nc.tensor.matmul(to, ones, member[:, j, :], start=(j == 0), stop=False)
                ins = nc.tensor.matmul(to, const("tri"), member[:, i, :], start=(i == 0), stop=True)
            ins.then_inc(s_rank, 1)
            pe.wait_ge(s_tab, 1)
            nb = pe.value_load(tab_i[0:1, N_BLOCKS:N_BLOCKS + 1], min_val=T * TOPK // P, max_val=N_BLOCKS)

            def turn(src, dst, signal):
                for c in range(4):
                    ins = nc.tensor.transpose(dst[:, P * c:P * c + P], src[:, P * c:P * c + P], ident)
                ins.then_inc(signal, 1)

            pe.wait_ge(s_hc, TT)
            pe.wait_ge(s_sel, 1)
            for m in range(2):
                if m:
                    pe.wait_ge(s_xtc, 1)
                for c in range(4):
                    for i in range(TT):
                        ins = nc.tensor.matmul(PT[:, P * c:P * c + P], hr[:, i, P * (4 * m + c):P * (4 * m + c) + P], select[:, i, :],
                                               start=(i == 0), stop=(i == TT - 1))
                ins.then_inc(s_xtp, 1)
            with pe.Fori(0, nb) as b:
                pe.wait_ge(s_xtc, b * 2 + 2)
                for hf in range(2):
                    for k in range(DC):
                        t = 8 * hf + k
                        pe.wait_ge(s_w[t], b * 16 + 16)
                        for j in range(2):
                            ins = nc.tensor.matmul(jb[2 * hf + j], xTb[:, k, :], mw[:, t, 512 * j:512 * j + 512],
                                                   start=(k == 0), stop=(k == DC - 1))
                        ins.then_inc(s_used, 1)
                pe.wait_ge(s_actr, b * 2 + 1)
                turn(actb[:, 0:512], PT, s_atp)
                pe.wait_ge(s_y, b + 1)
                for k in range(DC):
                    if k == 0:
                        pe.wait_ge(s_atc, b * 2 + 1)
                    if k == 4:
                        pe.wait_ge(s_actr, b * 2 + 2)
                        turn(actb[:, 512:1024], PO, s_atp)
                        pe.wait_ge(s_ga, b * 16 + 16)
                        turn(xg[:, 0:512], PT, s_xtp)
                        pe.wait_ge(s_atc, b * 2 + 2)
                    if k == 6:
                        pe.wait_ge(s_xtc, b * 2 + 3)
                        turn(xg[:, 512:1024], PT, s_xtp)
                    pe.wait_ge(s_w[16 + k], b * 16 + 16)
                    for j in range(2):
                        ins = nc.tensor.matmul(S[:, 512 * j:512 * j + 512], aT[:, k, :], mw[:, 16 + k, 512 * j:512 * j + 512],
                                               start=(k == 0), stop=(k == DC - 1))
                    ins.then_inc(s_used, 1)
            pe.wait_ge(s_y, nb + 1)
            for i in range(TT):
                pe.wait_ge(s_acc, TOPK * i + TOPK)
                if i:
                    pe.wait_ge(s_tTc, i)
                for c in range(DC):
                    ins = nc.tensor.transpose(S[:, P * c:P * c + P], acc[:, i, P * c:P * c + P], ident)
                ins.then_inc(s_tT, 1)
            norm("final")

        @block.scalar
        def _(act):
            steps = [0]

            def link(ins):
                steps[0] += 1
                ins.then_inc(s_act, 1)
                act.wait_ge(s_act, steps[0])

            copied = [0]

            def evacuate(stage):
                evacuate_to(stages[stage][1])

            def evacuate_to(b):
                a, copied[0] = copied[0], b
                for n in range(a, b):
                    act.wait_ge(s_pair, n + 1)
                    for m, (dst, func, scale, bias, rows, cols) in enumerate(pairs[n][1]):
                        src = jb[2 * (n % 2) + m][0:rows, 0:cols]
                        if len(dst.shape) == 3:
                            src = v3(src, dst.shape[1])
                        ins = nc.scalar.activation(dst, src, func, bias=bias, scale=scale)
                    ins.then_inc(s_evac, 1)

            def norm_root(name):
                n = NI[name]
                w = NORMS[n][3]
                act.wait_ge(s_ms, n + 1)
                nc.scalar.activation(ms[:, 0:w], ms[:, 0:w], F.Sqrt).then_inc(s_rt, 1)

            def exps(u):
                U = UNITS[u]
                act.wait_ge(s_max, u + 1)
                src = masked[:, 0:U["nk"]] if U["mask"] is not None else S[:, 0:U["nk"]]
                scale = 1.0 if U["mask"] is not None else U["scale"]
                nc.scalar.activation(U["pr"][:, u % 2, 0:U["nk"]], src, F.Exp, bias=small[:, u % 2:u % 2 + 1], scale=scale,
                                     accum_out=small[:, 2 + u % 2:3 + u % 2]).then_inc(s_exp, 1)

            def attention(a, b, stage=None, weights=None):
                exps(a)
                for u in range(a, b):
                    U = UNITS[u]
                    nv = len(U["v"])
                    if stage:
                        evacuate_to(filled(stage, weights, 2 * (u - a))[1])
                    for g in range((nv + 3) // 4):
                        w = P * min(4, nv - 4 * g)
                        act.wait_ge(s_tr, turns0[u] + g + 1)
                        nc.scalar.activation(U["pt"][:, 512 * g:512 * g + w], PT[:, 0:w], F.Copy).then_inc(s_trc, 1)
                    if u + 1 < b:
                        exps(u + 1)
                    if stage:
                        evacuate_to(filled(stage, weights, 2 * (u - a) + 1)[1])
                    act.wait_ge(s_pv, u + 1)
                    nc.scalar.activation(U["dst"], PO[U["rows"], 0:P], F.Copy).then_inc(s_out, 1)

            act.wait_ge(s_zero, 1)
            for half in range(2):
                act.dma_start(yrows[:, 512 * half:512 * half + 512].rearrange("(p b) n -> p b n", p=P),
                              zeros.unsqueeze(1).broadcast_to([P, N_ROWS // P, 512])).then_inc(s_yst, 16)
            norm_root("pre_mix")
            norm_root("mem")
            act.wait_ge(s_ang, 1)
            nc.scalar.activation(sinT, trn, F.Sin).then_inc(s_sin, 1)
            act.wait_ge(s_ang, 2)
            nc.scalar.activation(cosT, ang, F.Sin).then_inc(s_sin, 1)
            act.wait_ge(s_silc, 1)
            nc.scalar.activation(small[:, 16:32], vcol("c_2", 0, 16), F.Sigmoid).then_inc(s_silc, 1)
            evacuate("in1")
            attention(0, U_X, "side1", UNIT32)
            attention(U_X, U_M, "mod", UNIT16)
            for n in ("attn", "conv", "xattn"):
                norm_root(n)
            evacuate("out1")
            norm_root("post_mix")
            norm_root("pre_mlp")
            evacuate("up")
            evacuate("down")
            norm_root("post_mlp")
            if stop == "x1":
                return
            norm_root("mix2")
            evacuate("in2q")
            norm_root("ctx")
            evacuate("in2")
            for n in ("qin", "ckv_lat", "ckv_ctx"):
                norm_root(n)
            evacuate("mla0")
            for g in range(4):
                attention(U_M + 8 * g, U_M + 8 * g + 8, f"mla{g + 1}" if g < 3 else None, UNIT8)
            act.wait_ge(s_lb, 1)
            nc.scalar.activation(small[:, 96:128], small[:, 96:128], F.Exp).then_inc(s_lbe, 1)
            evacuate("hg0")
            for n in range(8):
                m = n % 2

                def drain(i):
                    if n < 7:
                        if i == 0 and n:
                            act.wait_ge(s_hg, n)
                        evacuate_to(filled(f"hg{n + 1}", HEAD_SLOTS, i)[1])

                nc.scalar.activation(E[:, 0, 0:T], hq[:, m, :], F.Sigmoid)
                nc.scalar.activation(E[:, 1, 0:T], hg[:, m, :], F.Sigmoid).then_inc(s_sil, 1)
                for d in range(2):
                    act.wait_ge(s_f, 2 * n + d + 1)
                    nc.scalar.activation(lnA, lnA, F.Ln)
                    z = zs[:, 2 * d + m, :]
                    nc.scalar.activation(z, z, F.Ln).then_inc(s_ln, 1)
                    act.wait_ge(s_cum, 2 * n + d + 1)
                    nc.scalar.activation(E[:, d, :], dlt[:, d, :], F.Exp, scale=-1.0)
                    nc.scalar.activation(X[:, d, :], cum[:, d, 0:T], F.Exp)
                    ends = v3(cum[:, d, :], AC)[:, :, P - 1 if d == 0 else 0]
                    nc.scalar.activation(el[:, d, :], ends, F.Exp).then_inc(s_ec, 1)
                    drain(2 * d)
                    act.wait_ge(s_kt, 2 * n + d + 1)
                    nc.scalar.activation(kT.rearrange("p a b -> p (a b)"), S[:, 0:TA], F.Copy).then_inc(s_ktc, 1)
                    drain(2 * d + 1)
                for L in range(14):
                    l = 14 * n + L
                    act.wait_ge(s_d, l + 1)
                    if L >= 2:
                        act.wait_ge(s_x, 15 * n + L - 1)
                    hf = level_half[L % LEVELS]
                    fwd = L < LEVELS
                    dv = dlt[:, L % 2, 0:T].rearrange("p (b s) -> p b s", s=2 * hf)
                    ev = E[:, L % 2, 0:T].rearrange("p (b s) -> p b s", s=2 * hf)
                    up, lo = slice(hf, 2 * hf), slice(0, hf)
                    qh, kh = (up, lo) if fwd else (lo, up)
                    nc.scalar.activation(ev[:, :, qh], dv[:, :, qh], F.Exp)
                    nc.scalar.activation(ev[:, :, kh], dv[:, :, kh], F.Exp, scale=-1.0).then_inc(s_e, 1)
                    if L:
                        drain(3 + L)
                drain(17)
                act.wait_ge(s_o, n + 1)
                nc.scalar.activation(osb, PO[:, :], F.Copy).then_inc(s_osb, 1)
                drain(18)
                norm_root(f"head{n}")
            evacuate("out2")
            if dbg is not None:
                return
            norm_root("ffn2")
            act.wait_ge(s_top, 1)
            for i in range(TT):
                ins = nc.scalar.activation(prob[:, 4 * i:4 * i + 4], top8[:, i, 0:4], F.Exp, bias=small[:, 144 + i:145 + i],
                                           accum_out=small[:, 148 + i:149 + i])
            ins.then_inc(s_tope, 1)
            for i in range(TT):
                act.wait_ge(s_hT, i + 1)
                nc.scalar.activation(hr[:, i, :], S[:, :], F.Copy).then_inc(s_hc, 1)
            act.wait_ge(s_tab, 1)
            nb = act.value_load(tab_i[0:1, N_BLOCKS:N_BLOCKS + 1], min_val=T * TOPK // P, max_val=N_BLOCKS)

            def copy_turned(n, src, at, signal_in, signal, dst):
                act.wait_ge(signal_in, n)
                d = dst.rearrange("p a b -> p (a b)")[:, 512 * at:512 * at + 512]
                nc.scalar.activation(d, src[:, :], F.Copy).then_inc(signal, 1)

            copy_turned(1, PT, 0, s_xtp, s_xtc, xTb)
            copy_turned(2, PT, 1, s_xtp, s_xtc, xTb)
            with act.Fori(0, nb) as b:
                act.wait_ge(s_glu, b * 2 + 1)
                nc.scalar.activation(sig, glu, F.Sigmoid, scale=1.702).then_inc(s_sig, 1)
                copy_turned(b * 2 + 1, PT, 0, s_atp, s_atc, aT)
                act.wait_ge(s_glu, b * 2 + 2)
                nc.scalar.activation(sig, glu, F.Sigmoid, scale=1.702).then_inc(s_sig, 1)
                copy_turned(b * 2 + 2, PO, 1, s_atp, s_atc, aT)
                copy_turned(b * 2 + 3, PT, 0, s_xtp, s_xtc, xTb)
                copy_turned(b * 2 + 4, PT, 1, s_xtp, s_xtc, xTb)
                act.wait_ge(s_y, b + 2)
                act.dma_start(yrows[bass.ds(b * P, P), :], yb).then_inc(s_yst, 16)
            for i in range(TT):
                act.wait_ge(s_tT, i + 1)
                nc.scalar.activation(yT[:, :, P * i:P * i + P], v3(S[:, :], DC), F.Copy).then_inc(s_tTc, 1)
            norm_root("final")

        @block.vector
        def _(dve):
            steps = [0]
            V = nc.vector

            def link(ins):
                steps[0] += 1
                ins.then_inc(s_vec, 1)
                dve.wait_ge(s_vec, steps[0])

            def norm_stats(name, stage=None):
                n = NI[name]
                _, src, nch, w = NORMS[n]
                for c in range(nch):
                    g = chunk0[n] + c
                    if stage:
                        dve.wait_ge(s_evac, stages[stage][0] + c // 2 + 1)
                    if g >= 2:
                        dve.wait_ge(s_mm, g - 1)
                    V.tensor_tensor(sq[:, g % 2, 0:w], src[:, c, 0:w], src[:, c, 0:w], ALU.mult).then_inc(s_sq, 1)
                dve.wait_ge(s_mm, chunk0[n] + nch)
                V.tensor_scalar(ms[:, 0:w], PT[:, 0:w], 1.0 / (P * nch), EPS, ALU.mult, ALU.add).then_inc(s_ms, 1)
                dve.wait_ge(s_rt, n + 1)
                link(V.reciprocal(rstd[:, 0:w], ms[:, 0:w]))

            def norm_apply(name, dst, gain):
                _, src, nch, w = NORMS[NI[name]]
                for c in range(nch):
                    V.scalar_tensor_tensor(dst[:, c, 0:w], src[:, c, 0:w], gain(c), rstd[:, 0:w], ALU.mult,
                                           ALU.mult).then_inc(s_norm, 1)

            def norm(name, dst, vname, stage=None):
                norm_stats(name, stage)
                norm_apply(name, dst, lambda c: vcol(vname, c))

            def rope(r):
                buf, co, si, rows = ROPES[r]
                dve.wait_ge(s_rot, r + 1)
                if r:
                    dve.wait_ge(s_rope, r)
                t = tmp2 if r >= 8 else ang
                link(V.tensor_tensor(t[0:rows, :], LB[r % 2][0:rows, :], si, ALU.mult))
                link(V.tensor_tensor(buf, buf, co, ALU.mult))
                V.tensor_tensor(buf, buf, t[0:rows, :], ALU.add).then_inc(s_rope, 1)

            def maxes(u):
                U = UNITS[u]
                dve.wait_ge(s_sc, u + 1)
                nk = U["nk"]
                nm = small[:, u % 2:u % 2 + 1]
                if U["mask"] is not None:
                    link(V.scalar_tensor_tensor(masked[:, 0:nk], S[:, 0:nk], U["scale"], U["mask"], ALU.mult, ALU.add))
                    link(V.tensor_reduce(nm, masked[:, 0:nk], AX.X, ALU.max))
                    V.tensor_scalar(nm, nm, -1.0, None, ALU.mult).then_inc(s_max, 1)
                else:
                    link(V.tensor_reduce(nm, S[:, 0:nk], AX.X, ALU.max))
                    V.tensor_scalar(nm, nm, -U["scale"], None, ALU.mult).then_inc(s_max, 1)

            def attention(a, b):
                maxes(a)
                for u in range(a, b):
                    U = UNITS[u]
                    dve.wait_ge(s_exp, u + 1)
                    link(V.reciprocal(small[:, 4:5], small[:, 2 + u % 2:3 + u % 2]))
                    pr = U["pr"][:, u % 2, 0:U["nk"]]
                    V.tensor_scalar(pr, pr, small[:, 4:5], None, ALU.mult).then_inc(s_prob, 1)
                    if u + 1 < b:
                        maxes(u + 1)

            dve.wait_ge(s_const, 32)
            V.memset(small[:, 10:11], 0.0).then_inc(s_silc, 1)
            dve.wait_ge(s_in, 16)
            norm("pre_mix", h, "g_pre_mix")
            dve.wait_ge(s_tok, 16)
            norm("mem", hm, "g_mem")
            dve.wait_ge(s_pos, 16)
            link(V.tensor_copy(cosT, ang.bitcast(i32)))
            link(V.tensor_scalar(cosT, cosT, const("inv_freq"), None, ALU.mult))
            magic = 12582912.0
            link(V.tensor_scalar(sinT, cosT, 1.0 / (2 * np.pi), magic, ALU.mult, ALU.add))
            link(V.tensor_scalar(sinT, sinT, -magic, None, ALU.add))
            link(V.scalar_tensor_tensor(trn, sinT, -6.28125, cosT, ALU.mult, ALU.add))
            link(V.scalar_tensor_tensor(trn, sinT, -0.0019350051879882812, trn, ALU.mult, ALU.add))
            link(V.scalar_tensor_tensor(trn, sinT, -3.019916050561733e-07, trn, ALU.mult, ALU.add))
            PI = 3.1415925
            link(V.tensor_scalar(ang, trn, float(np.pi / 2), -2 * float(np.pi), ALU.is_gt, ALU.mult))
            link(V.scalar_tensor_tensor(ang, trn, float(np.pi / 2), ang, ALU.add, ALU.add))
            link(V.tensor_scalar(ang, ang, PI, -PI, ALU.min, ALU.max))
            V.tensor_scalar(trn, trn, PI, -PI, ALU.min, ALU.max).then_inc(s_ang, 2)
            dve.wait_ge(s_silc, 2)
            for j, nm in enumerate(("c_2", "c_ctx_2")):
                ins = V.tensor_tensor(v3(cs, 8)[:, :, j], small[:, 16 + 8 * j:24 + 8 * j], vcol(nm, 0, 8), ALU.mult)
            ins.then_inc(s_silu, 1)
            dve.wait_ge(s_sin, 2)
            dve.wait_ge(s_evac, stages["in1"][1])
            V.memset(small[:, 8:9], 0.0).then_inc(s_rot_in, 1)
            for r in range(8):
                rope(r)
            attention(0, U_X)
            dve.wait_ge(s_evac, stages["side1"][1])
            for c in range(2):
                w = lambda tap: vcol("conv_w", 2 * tap + c)
                link(V.tensor_tensor(cc[:, c, :], cc[:, c, :], cu[:, c, :], ALU.mult))
                z, y = cc[:, c, :], yconv[:, c, :]
                link(V.tensor_scalar(y, z, w(2), None, ALU.mult))
                link(V.scalar_tensor_tensor(y[:, 1:T], z[:, 0:T - 1], w(1), y[:, 1:T], ALU.mult, ALU.add))
                link(V.scalar_tensor_tensor(y[:, 2:T], z[:, 0:T - 2], w(0), y[:, 2:T], ALU.mult, ALU.add))
                link(V.tensor_tensor(y, y, cb[:, c, :], ALU.mult))
            attention(U_X, U_M)
            dve.wait_ge(s_modt, 1)
            V.tensor_tensor(modv, v3(PT[:, 0:96], 48), vcol("b_mod_2", 0, 48).unsqueeze(2).broadcast_to([P, 48, 2]),
                            ALU.add).then_inc(s_modr, 1)
            dve.wait_ge(s_out, U_M)
            norm("attn", h[:, 0:4, :], "g_attn_out")
            norm("conv", h[:, 4:6, :], "g_conv_out")
            norm("xattn", h[:, 6:8, :], "g_xattn_out")
            def add_normed(name, gain, stage):
                norm_stats(name, stage)
                _, src, nch, w = NORMS[NI[name]]
                for c in range(nch):
                    link(V.scalar_tensor_tensor(src[:, c, :], src[:, c, :], gain(c), rstd[:, :], ALU.mult, ALU.mult))
                    link(V.tensor_tensor(x[:, c, :], x[:, c, :], src[:, c, :], ALU.add))

            add_normed("post_mix", lambda c: vcol("g_post_mix", c), "out1")
            norm("pre_mlp", h, "g_pre_mlp")
            for i in range(16):
                dve.wait_ge(s_evac, stages["up"][0] + i + 1)
                f = ffn[:, 2 * i:2 * i + 2, :]
                V.tensor_tensor(f, f, f, ALU.mult).then_inc(s_ffn, 1)
            add_normed("post_mlp", lambda c: vcol("g_post_mlp", c), "down")
            V.memset(small[:, 8:9], 0.0).then_inc(s_res, 1)
            if stop == "x1":
                return
            gm = small[:, 32:56].rearrange("p (a b) -> p a b", a=3)
            for j, (part, who, nm) in enumerate(((1, 0, "norm_mix_g_2"), (1, 1, "norm_mix_g_2"), (4, 0, "norm_ffn_g_2"))):
                link(V.scalar_tensor_tensor(gm[:, j, :], modv[:, 8 * part:8 * part + 8, who], 1.0, vcol(nm, 0, 8), ALU.add, ALU.mult))

            def modulated(name, dst, j, shift, who):
                norm_stats(name)
                _, src, nch, w = NORMS[NI[name]]
                for c in range(nch):
                    link(V.scalar_tensor_tensor(dst[:, c, 0:w], src[:, c, 0:w], gm[:, j, c:c + 1], rstd[:, 0:w], ALU.mult, ALU.mult))
                    V.tensor_scalar(dst[:, c, 0:w], dst[:, c, 0:w], modv[:, 8 * shift + c, who:who + 1], None,
                                    ALU.add).then_inc(s_norm, 1)

            modulated("mix2", ha, 0, 0, 0)
            dve.wait_ge(s_tok, 32)
            modulated("ctx", hctx, 1, 0, 1)
            norm("qin", qin, "mla_q_norm_g_2", "in2q")
            dve.wait_ge(s_evac, stages["in2"][1])
            norm("ckv_lat", ckv, "mla_kv_norm_g_2")
            norm("ckv_ctx", ckv[:, :, T:TA], "mla_kv_norm_g_2")
            rope(8)
            for g in range(4):
                dve.wait_ge(s_evac, stages[f"mla{g}"][1])
                for m in range(2):
                    rope(9 + 2 * g + m)
                attention(U_M + 8 * g, U_M + 8 * g + 8)
            lbv = vcol("hg_lb_logits_2", 0, 32).rearrange("p (d l c) -> p d l c", d=2, l=2)
            lbe = small[:, 96:128].rearrange("p (d l c) -> p d l c", d=2, l=2)
            lb = small[:, 128:144].rearrange("p (d c) -> p d c", d=2)
            olb = small[:, 56:72].rearrange("p (d c) -> p d c", d=2)
            link(V.tensor_tensor(lb, lbv[:, :, 0, :], lbv[:, :, 1, :], ALU.max))
            link(V.tensor_tensor(lbe[:, :, 0, :], lbv[:, :, 0, :], lb, ALU.subtract))
            V.tensor_tensor(lbe[:, :, 1, :], lbv[:, :, 1, :], lb, ALU.subtract).then_inc(s_lb, 1)
            dve.wait_ge(s_lbe, 1)
            link(V.tensor_tensor(olb, lbe[:, :, 0, :], lbe[:, :, 1, :], ALU.add))
            link(V.reciprocal(olb, olb))
            link(V.tensor_tensor(lb, lbe[:, :, 0, :], olb, ALU.mult))
            link(V.tensor_scalar(olb, lb, -1.0, 1.0, ALU.mult, ALU.add))

            def merge(n):
                m = n % 2
                dve.wait_ge(s_osb, n + 1)
                norm_stats(f"head{n}")
                link(V.scalar_tensor_tensor(osb, osb, vcol("hg_norm_g_2"), rstd[:, :], ALU.mult, ALU.mult))
                link(V.tensor_tensor(osb, osb, hg[:, m, :], ALU.mult))
                link(V.tensor_tensor(osb, osb, s8[:, m, :], ALU.mult))
                link(V.tensor_tensor(ymla[:, n, :], ymla[:, n, :], s7[:, m, :], ALU.mult))
                V.tensor_tensor(ymla[:, n, :], ymla[:, n, :], osb, ALU.add).then_inc(s_hg, 1)

            for n in range(8):
                    m = n % 2
                    dve.wait_ge(s_evac, stages[f"hg{n}"][1])
                    dve.wait_ge(s_sil, n + 1)
                    link(V.scalar_tensor_tensor(qq, hq[:, m, :], P ** -0.5, E[:, 0, 0:T], ALU.mult, ALU.mult))
                    link(V.tensor_tensor(hg[:, m, :], hg[:, m, :], E[:, 1, 0:T], ALU.mult))
                    for d in range(2):
                        z = zs[:, 2 * d + m, :]
                        link(V.tensor_scalar(z, z, olb[:, d, n:n + 1], lb[:, d, n:n + 1], ALU.mult, ALU.add))
                        V.tensor_scalar(kk[:, d, :], z, -1.0, 1.0, ALU.mult, ALU.add)
                        link(V.tensor_scalar(lnA, z, 2.0 ** -63, None, ALU.max))
                        V.tensor_scalar(z, z, 2.0 ** 63, 1.0, ALU.mult, ALU.min).then_inc(s_f, 1)
                        dve.wait_ge(s_ln, 2 * n + d + 1)
                        link(V.tensor_tensor(z, z, lnA, ALU.add))
                        cd = cum[:, d, :]
                        if d == 0:
                            link(V.tensor_tensor_scan(cd, const("reset"), z, 0.0, ALU.mult, ALU.add))
                        else:
                            link(V.tensor_tensor_scan(cd[:, ::-1], const("reset"), z[:, ::-1], 0.0, ALU.mult, ALU.add))
                        c3 = v3(cd, AC)
                        far = c3[:, :, P - 1:P] if d == 0 else c3[:, :, 0:1]
                        V.tensor_tensor(v3(dlt[:, d, :], AC), c3, far.broadcast_to([P, AC, P]), ALU.subtract).then_inc(s_cum, 1)
                        dve.wait_ge(s_ec, 2 * n + d + 1)
                        V.tensor_tensor(qe[:, d, :], qq, X[:, d, :], ALU.mult)
                        V.tensor_tensor(E[:, d, :], E[:, d, :], kk[:, d, :], ALU.mult).then_inc(s_kd, 1)
                        dve.wait_ge(s_ds, 2 * n + d + 1)
                        link(V.tensor_copy(St[:, 5 * d, :], PT[:, 0:P]))
                        for j in range(1, 5):
                            src = PT[:, P * j:P * j + P] if j < 4 else LB[1][:, 256:384]
                            c = SEQ[d][j]
                            ins = V.scalar_tensor_tensor(St[:, 5 * d + j, :], St[:, 5 * d + j - 1, :], el[:, d, c:c + 1], src,
                                                         ALU.mult, ALU.add)
                            if j < 4:
                                link(ins)
                        ins.then_inc(s_st, 1)

                    def views(a, hf):
                        return a.rearrange("p (b s) -> p b s", s=2 * hf)

                    def gather(L):
                        dve.wait_ge(s_p, 15 * n + L + 1)
                        if 15 * n + L:
                            dve.wait_ge(s_at, 15 * n + L)
                        if L == 14:
                            mk = diagonal.unsqueeze(1).broadcast_to([P, TT, P])
                            V.copy_predicated(v3(At, TT), mk, v3(LB[L % 2], TT)).then_inc(s_at, 1)
                            return
                        hf = level_half[L % LEVELS]
                        to = At.rearrange("p (c b s) -> p c b s", c=TT, s=2 * hf)
                        to = to[:, :, :, hf:2 * hf] if L < LEVELS else to[:, :, :, 0:hf]
                        mk = level_masks[:, L:L + 1, :].broadcast_to([P, TT, 64]).rearrange("p c (b s) -> p c b s", s=hf)
                        V.copy_predicated(to, mk, LB[L % 2][:, 0:256].rearrange("p (c b s) -> p c b s", c=TT, s=hf)).then_inc(s_at, 1)

                    for L in range(14):
                        dve.wait_ge(s_e, 14 * n + L + 1)
                        hf, d = level_half[L % LEVELS], L // LEVELS
                        up, lo = slice(hf, 2 * hf), slice(0, hf)
                        qh, kh = (up, lo) if d == 0 else (lo, up)
                        ev, xv = views(E[:, L % 2, 0:T], hf), views(X[:, L % 2, :], hf)
                        V.tensor_tensor(xv[:, :, qh], ev[:, :, qh], views(qq, hf)[:, :, qh], ALU.mult)
                        V.tensor_tensor(xv[:, :, kh], ev[:, :, kh], views(kk[:, d, 0:T], hf)[:, :, kh], ALU.mult).then_inc(s_x, 1)
                        if L >= 1:
                            gather(L - 1)
                    V.memset(small[:, 8:9], 0.0).then_inc(s_x, 1)
                    gather(13)
                    gather(14)
                    merge(n)
            dve.wait_ge(s_evac, stages["out2"][1])
            for c in range(DC):
                ins = V.scalar_tensor_tensor(x[:, c, :], mout2[:, c, :], modv[:, 16 + c, 0:1], x[:, c, :], ALU.mult, ALU.add)
                if c < DC - 1:
                    link(ins)
            ins.then_inc(s_res, 1)
            if dbg is not None:
                return
            dve.wait_ge(s_res, 2)
            modulated("ffn2", h3, 2, 3, 0)
            dve.wait_ge(s_lgp, 1)
            link(V.tensor_copy(lg, v3(PO[:, 0:TT * N_EXP], TT)))
            for i in range(TT):
                link(V.max(top8[:, i, :], lg[:, i, :]))
                link(V.max_index(idx8.bitcast(mybir.dt.uint32)[:, i, :], top8[:, i, :], lg[:, i, :]))
            V.tensor_scalar(small[:, 144:148], top8[:, :, 0], -1.0, None, ALU.mult).then_inc(s_top, 1)
            link(V.tensor_copy(idxf, idx8.bitcast(mybir.dt.uint32)[:, :, 0:4]))
            hot3 = hot.rearrange("p (a e) -> p a e", e=N_EXP)
            en = const("expert_no").unsqueeze(1).broadcast_to([P, 16, N_EXP])
            i3 = idxf.rearrange("p a b -> p (a b)").unsqueeze(2).broadcast_to([P, 16, N_EXP])
            link(V.tensor_tensor(hot3, en, i3, ALU.is_equal))
            V.tensor_reduce(member, hot.rearrange("p (i k e) -> p i e k", i=TT, k=TOPK), AX.X, ALU.add).then_inc(s_mem, 1)
            dve.wait_ge(s_cnt, 1)
            link(V.tensor_scalar(blocks_of, PT[:, 0:N_EXP], 1.0 / P, (P - 1) / (2.0 * P), ALU.mult, ALU.add))
            link(V.tensor_scalar(blocks_of, blocks_of, magic, -magic, ALU.add, ALU.add))
            link(V.tensor_tensor_scan(block_end, ones[:, 0:N_EXP], blocks_of, 0.0, ALU.mult, ALU.add))
            cm = cmpb[0:1, :].rearrange("p (b e) -> p b e", e=N_EXP)
            link(V.tensor_tensor(cm, block_end[0:1, :].unsqueeze(1).broadcast_to([1, N_BLOCKS, N_EXP]),
                                 const("block_no")[0:1, :].unsqueeze(2).broadcast_to([1, N_BLOCKS, N_EXP]), ALU.is_le))
            link(V.tensor_reduce(block_expert[0:1, :], cm, AX.X, ALU.add))
            link(V.tensor_scalar(tab_i[0:1, 0:N_BLOCKS], block_expert[0:1, :], float(N_EXP - 1), None, ALU.min))
            V.tensor_copy(tab_i[0:1, N_BLOCKS:N_BLOCKS + 1], block_end[0:1, N_EXP - 1:N_EXP]).then_inc(s_tab, 1)
            link(V.tensor_tensor(first_row, block_end, blocks_of, ALU.subtract))
            link(V.tensor_scalar(first_row, first_row, float(P), None, ALU.mult))
            dve.wait_ge(s_rank, 1)
            link(V.tensor_tensor(rank, v3(PO[:, 128:128 + TT * N_EXP], TT), first_row.unsqueeze(1).broadcast_to([P, TT, N_EXP]), ALU.add))
            for i in range(TT):
                a = hot2.rearrange("p (i k e) -> p i k e", i=TT, k=TOPK)[:, i]
                h_ = hot.rearrange("p (i k e) -> p i k e", i=TT, k=TOPK)[:, i]
                link(V.tensor_tensor(a, h_, rank[:, i:i + 1, :].broadcast_to([P, TOPK, N_EXP]), ALU.mult))
            link(V.tensor_reduce(destf, hot2.rearrange("p (a e) -> p a e", e=N_EXP), AX.X, ALU.add))
            link(V.tensor_copy(tokno.bitcast(i32), const("token_no")))
            V.tensor_copy(desti.bitcast(i32), destf).then_inc(s_dest, 1)
            dve.wait_ge(s_dest, 1)
            for k in range(TOPK):
                for i in range(TT):
                    j = TOPK * i + k
                    if k == 0:
                        ins = V.tensor_scalar(select[:, i, :], const("row_no"), destf[:, j:j + 1], None, ALU.is_equal)
                    else:
                        ins = V.scalar_tensor_tensor(select[:, i, :], const("row_no"), destf[:, j:j + 1], select[:, i, :], ALU.is_equal, ALU.add)
                if k < TOPK - 1:
                    link(ins)
            ins.then_inc(s_sel, 1)
            dve.wait_ge(s_tope, 1)
            link(V.reciprocal(small[:, 152:156], small[:, 148:152]))
            for i in range(TT):
                link(V.tensor_scalar(prob[:, 4 * i:4 * i + 4], prob[:, 4 * i:4 * i + 4], small[:, 152 + i:153 + i], None, ALU.mult))
            dve.wait_ge(s_tab, 1)
            nb = dve.value_load(tab_i[0:1, N_BLOCKS:N_BLOCKS + 1], min_val=T * TOPK // P, max_val=N_BLOCKS)
            LOOP_STEPS = 5
            V.memset(small[:, 9:10], 0.0).then_inc(s_y, 1)
            with dve.Fori(0, nb) as b:
                done = [0]

                def step(ins):
                    done[0] += 1
                    ins.then_inc(s_vl, 1)
                    dve.wait_ge(s_vl, b * LOOP_STEPS + done[0])

                dve.wait_ge(s_bb, b + 1)
                for hf in range(2):
                    dve.wait_ge(s_used, b * MT + 8 * (hf + 1))
                    step(V.tensor_tensor(tbuf, G[:, 1024 * hf:1024 * hf + 1024], biasb[:, 1024 * hf:1024 * hf + 1024], ALU.add))
                    pr = tbuf.rearrange("p (n two) -> p n two", two=2)
                    V.tensor_scalar(glu, pr[:, :, 0], 7.0, None, ALU.min).then_inc(s_glu, 1)
                    step(V.tensor_scalar(lin, pr[:, :, 1], 7.0, -7.0, ALU.min, ALU.max))
                    dve.wait_ge(s_glu, b * 2 + hf + 1)
                    a = actb[:, 512 * hf:512 * hf + 512]
                    V.scalar_tensor_tensor(lin, lin, 1.0, glu, ALU.add, ALU.mult).then_inc(s_lg, 1)
                    dve.wait_ge(s_lg, b * 2 + hf + 1)
                    dve.wait_ge(s_sig, b * 2 + hf + 1)
                    V.tensor_tensor(a, lin, sig, ALU.mult).then_inc(s_actr, 1)
                    dve.wait_ge(s_actr, b * 2 + hf + 1)
                dve.wait_ge(s_used, b * MT + MT)
                dve.wait_ge(s_yst, b * 16 + 32)
                step(V.tensor_tensor(yb, S[:, :], biasb[:, 2048:3072], ALU.add))
                V.memset(small[:, 9:10], 0.0).then_inc(s_y, 1)
                dve.wait_ge(s_y, b + 2)
            def residual(i):
                dve.wait_ge(s_tTc, i + 1)
                ts = slice(P * i, P * i + P)
                link(V.tensor_tensor(yT[:, :, ts], yT[:, :, ts], modv[:, 40:48, 0:1].broadcast_to([P, DC, P]), ALU.mult))
                link(V.tensor_tensor(x[:, :, ts], x[:, :, ts], yT[:, :, ts], ALU.add))

            for i in range(TT):
                if i >= 2:
                    residual(i - 2)
                for k in range(TOPK):
                    j = TOPK * i + k
                    dve.wait_ge(s_yg[j % YBUF], 16 * (j // YBUF + 1))
                    w = prob[:, j:j + 1]
                    if k == 0:
                        V.tensor_scalar(acc[:, i, :], yg[:, j % YBUF, :], w, None, ALU.mult).then_inc(s_acc, 1)
                    else:
                        dve.wait_ge(s_acc, j)
                        V.scalar_tensor_tensor(acc[:, i, :], yg[:, j % YBUF, :], w, acc[:, i, :], ALU.mult, ALU.add).then_inc(s_acc, 1)
            residual(2)
            residual(3)
            norm("final", fin, "final_norm_g_2")


def constants():
    c = np.zeros((P, N_CONST), np.float32)

    def put(name, a):
        c[:, CONST_AT[name]:CONST_AT[name] + dict(CONSTS)[name]] = a

    put("ident", np.eye(P, dtype=np.float32))
    put("ones", 1.0)
    r = np.zeros((P, P), np.float32)
    for b in (0, 64):
        for i in range(32):
            r[b + i + 32, b + i] = -1.0
            r[b + i, b + i + 32] = 1.0
    put("rot", r)
    d = np.arange(P)[:, None] + (T - P) - np.arange(T)[None, :]
    n = ((d >= 0) & (d <= 128)).astype(int) + ((d >= 0) & (d % 4 == 0)) + ((d >= 0) & (d % 16 == 0))
    put("band", np.where(n > 0, np.log(np.maximum(n, 1)), NEG))
    put("row_no", np.arange(P)[None, :])
    lv = np.zeros((P, 14, P // 2), np.uint8)
    s, t = np.arange(P)[:, None], np.arange(P)[None, :]
    for i in range(LEVELS):
        hf = P >> (i + 1)
        same = (s // (2 * hf)) == (t // (2 * hf))
        forward = same & (s % (2 * hf) < hf) & (t % (2 * hf) >= hf)
        upper = np.arange(P) % (2 * hf) >= hf
        lv[:, i] = forward[:, upper]
        lv[:, LEVELS + i] = forward.T[:, ~upper]
    put("diagonal", (s == t).astype(np.uint8).view(np.float32))
    put("levels", lv.reshape(P, -1).view(np.float32))
    put("reset", (np.arange(TA) % P != 0).astype(np.float32))
    half = DH1 // 2
    inv = np.float32(10000.0) ** (-(np.arange(half, dtype=np.float32) * np.float32(2.0) / np.float32(DH1)))
    put("inv_freq", np.tile(inv.astype(np.float32), 4)[:, None])
    row, col = np.repeat(np.arange(T // 64), 64).astype(np.float32), np.tile(np.arange(64), T // 64).astype(np.float32)
    ax = np.float32(10000.0) ** (-np.arange(16, dtype=np.float32) / np.float32(16))
    a = np.concatenate([row[:, None] * ax, col[:, None] * ax], axis=1).T
    put("axial_cos", np.tile(np.cos(a), (4, 1)))
    put("axial_sin", np.tile(np.sin(a), (4, 1)))
    put("tri", (s < t).astype(np.float32))
    put("expert_no", np.arange(N_EXP)[None, :])
    put("block_no", np.arange(N_BLOCKS)[None, :])
    put("token_no", (np.arange(P)[:, None] + P * np.arange(TT)[None, :]))
    return c


def lay_out(inp):
    def fm(a):
        a = np.asarray(a)
        return np.ascontiguousarray(a.T.reshape(-1, P, a.shape[0]).transpose(1, 0, 2))

    arr = {"xT": fm(inp["x"][0]), "memT": fm(inp["mem"][0]), "ctxT": fm(inp["ctx_2"][0])}
    v = np.zeros((P, N_VEC), np.float32)
    for name, k in VECS:
        v[:, VEC_AT[name]:VEC_AT[name] + k] = np.asarray(inp[name]).reshape(k, P).T
    arr["vecs"] = v
    w = np.zeros((NT, P, SLOT), np.float32)
    for t, (name, k0, kc, runs, n) in enumerate(WT):
        a = np.asarray(inp[name])[0][k0 * P:(k0 + kc) * P]
        a = np.concatenate([a[:, at:at + m] for at, m in runs], axis=1)
        w[t, :, 0:kc * n] = a.reshape(kc, P, n).transpose(1, 0, 2).reshape(P, kc * n)
    arr["wt"] = w
    arr["pos"] = np.ascontiguousarray(np.asarray(inp["positions"])[0])
    arr["wr"] = np.ascontiguousarray(np.asarray(inp["w_router_2"])[0].reshape(DC, P, N_EXP).transpose(1, 0, 2))
    arr["br"] = np.ascontiguousarray(np.asarray(inp["b_router_2"])[0][None, :])
    arr["wgu"] = np.asarray(inp["w_gate_up_2"])[0]
    arr["bgu"] = np.asarray(inp["b_gate_up_2"])[0]
    arr["wdn"] = np.asarray(inp["w_down_2"])[0]
    arr["bdn"] = np.asarray(inp["b_down_2"])[0]
    arr["consts"] = constants()
    return arr


ORDER = ["wt", "xT", "memT", "ctxT", "pos", "vecs", "consts", "wr", "br", "wgu", "bgu", "wdn", "bdn"]
DEBUG = None


def kernel(**inputs):
    import concourse.bacc as bacc
    from concourse.bass_utils import run_bass_kernel_spmd as run

    nc = bacc.Bacc("TRN2", target_bir_lowering=False, num_devices=1)
    arrays = {f"in_{k}": v for k, v in lay_out(inputs).items()}
    args = [nc.dram_tensor(f"in_{k}", arrays[f"in_{k}"].shape, mybir.dt.from_np(arrays[f"in_{k}"].dtype),
                           kind="ExternalInput").ap() for k in ORDER]
    f32, i32 = mybir.dt.float32, mybir.dt.int32
    out = nc.dram_tensor("outT", (P, DC, T), f32, kind="ExternalOutput").ap()
    hrows = nc.dram_tensor("h_rows", (T, D), f32).ap()
    tokof = nc.dram_tensor("token_of_row", (N_ROWS, 1), i32).ap()
    yrows = nc.dram_tensor("y_rows", (N_ROWS, D), f32).ap()
    blk = nc.dram_tensor("block_table", (1, 64), i32).ap()
    if DEBUG:
        build(nc, *args, out, hrows, tokof, yrows, blk, dbg=out, stop=DEBUG)
    else:
        build(nc, *args, out, hrows, tokof, yrows, blk)
    r = run(nc, [arrays], core_ids=[0])
    got = np.asarray(r.results[0]["outT"])
    return np.ascontiguousarray(got.transpose(1, 0, 2).reshape(D, T).T)[None]
```
